# Optimizing a Trainium2 kernel written in Bass

```python
import jax, jax.numpy as jnp
from jax import lax
import numpy as np

D_MODEL = 1024
BATCH = 1
SEQ = 256
DEPTH = 1
DEC_BATCH = 1
DEC_SEQ = 1024
PAST_LEN = 512

GRID_W = 64
D_MIX = D_MODEL
D_FOURIER = D_MIX // 2
N_FOURIER_GROUPS = 4
FOURIER_GROUP_W = D_FOURIER // N_FOURIER_GROUPS
D_RET = D_MIX - D_FOURIER
N_RET_HEADS = 4
HEAD_DIM = D_RET // N_RET_HEADS
CHUNK = 128
N_EXPERTS = 16
EC_CAPACITY_FACTOR = 2
D_EXPERT_FF = 2816
ROPE_BASE = 10000.0
EPS = 1e-6
D_IN_PROJ = D_FOURIER + 5 * D_RET
LOG_GAMMA_FWD = np.log(1.0 - 2.0 ** (-5.0 - np.arange(N_RET_HEADS))).astype(np.float32)
LOG_GAMMA_BWD = np.log(1.0 - 2.0 ** (-5.5 - np.arange(N_RET_HEADS))).astype(np.float32)

kernel_name = "hybrid_fnet_retention_ec_moe_diffusion_step"

def rmsnorm(x, g):
    xf = x.astype(jnp.float32)
    r = lax.rsqrt(jnp.mean(xf * xf, axis=-1, keepdims=True) + EPS)
    return (xf * r).astype(x.dtype) * g

def fourier_mix(u, w_fmix):
    b, n, _ = u.shape
    ug = u.reshape(b, n, N_FOURIER_GROUPS, FOURIER_GROUP_W).astype(jnp.float32)
    f = jnp.fft.fft2(ug, axes=(1, 3), norm="ortho").real.astype(u.dtype)
    y = jnp.einsum('bngw,gwv->bngv', f, w_fmix)
    return y.reshape(b, n, D_FOURIER)

def _rotate(t, ang):
    p = ang.shape[-1]
    cos = jnp.cos(ang)[None, :, None, :]
    sin = jnp.sin(ang)[None, :, None, :]
    t1, t2 = t[..., :p], t[..., p:]
    return jnp.concatenate([t1 * cos - t2 * sin, t1 * sin + t2 * cos], axis=-1)

def axial_rope(t):
    n = t.shape[1]
    rows_n = n // GRID_W
    row = jnp.repeat(jnp.arange(rows_n, dtype=jnp.float32), GRID_W)
    col = jnp.tile(jnp.arange(GRID_W, dtype=jnp.float32), rows_n)
    half = HEAD_DIM // 2
    n_pairs = half // 2
    freqs = ROPE_BASE ** (-jnp.arange(n_pairs, dtype=jnp.float32) / n_pairs)
    tr = _rotate(t[..., :half], row[:, None] * freqs[None, :])
    tc = _rotate(t[..., half:], col[:, None] * freqs[None, :])
    return jnp.concatenate([tr, tc], axis=-1)

def chunk_retention(q, k, v, log_gamma, s0):
    b, h, n, dh = q.shape
    nc = n // CHUNK
    lg = jnp.asarray(log_gamma)
    i = jnp.arange(CHUNK, dtype=jnp.float32)
    diff = i[:, None] - i[None, :]
    dmat = jnp.where(diff[None] >= 0, jnp.exp(lg[:, None, None] * jnp.maximum(diff, 0.0)[None]), 0.0)
    q_dec = jnp.exp(lg[:, None] * (i[None, :] + 1.0))
    k_dec = jnp.exp(lg[:, None] * (CHUNK - 1.0 - i[None, :]))
    s_dec = jnp.exp(lg * CHUNK)

    def split(t):
        return t.reshape(b, h, nc, CHUNK, dh).transpose(2, 0, 1, 3, 4)

    def step(s, qkv):
        qc, kc, vc = qkv
        att = jnp.einsum('bhid,bhjd->bhij', qc, kc) * dmat
        o = (jnp.einsum('bhij,bhje->bhie', att, vc)
             + jnp.einsum('bhid,bhde->bhie', qc * q_dec[:, :, None], s))
        s = s * s_dec[:, None, None] + jnp.einsum('bhjd,bhje->bhde', kc * k_dec[:, :, None], vc)
        return s, o

    s_end, o = lax.scan(step, s0, (split(q), split(k), split(v)))
    o = o.transpose(1, 2, 0, 3, 4).reshape(b, h, n, dh)
    return o, s_end

def head_groupnorm(o):
    mu = jnp.mean(o, axis=-1, keepdims=True)
    var = jnp.mean(jnp.square(o - mu), axis=-1, keepdims=True)
    return (o - mu) * lax.rsqrt(var + EPS)

def retention_mixer(p, s_fwd0, s_bwd0, use_rope):
    b, n, _ = p.shape
    q, k, v, gf, gb = jnp.split(p.astype(jnp.float32), 5, axis=-1)
    q = q.reshape(b, n, N_RET_HEADS, HEAD_DIM)
    k = k.reshape(b, n, N_RET_HEADS, HEAD_DIM)
    v = v.reshape(b, n, N_RET_HEADS, HEAD_DIM)
    if use_rope:
        q = axial_rope(q)
        k = axial_rope(k)
    k = k * (HEAD_DIM ** -0.5)
    q, k, v = (t.transpose(0, 2, 1, 3) for t in (q, k, v))
    of, sf = chunk_retention(q, k, v, LOG_GAMMA_FWD, s_fwd0)
    ob, sb = chunk_retention(jnp.flip(q, 2), jnp.flip(k, 2), jnp.flip(v, 2), LOG_GAMMA_BWD, s_bwd0)
    ob = jnp.flip(ob, 2)
    of = head_groupnorm(of).transpose(0, 2, 1, 3).reshape(b, n, D_RET)
    ob = head_groupnorm(ob).transpose(0, 2, 1, 3).reshape(b, n, D_RET)
    y = jax.nn.silu(gf) * of + jax.nn.silu(gb) * ob
    return y.astype(p.dtype), sf, sb

def ec_moe(h, w_router, w_gate, w_up, w_down):
    b, n, d = h.shape
    t = b * n
    ht = h.reshape(t, d)
    aff = jax.nn.softmax(ht.astype(jnp.float32) @ w_router.astype(jnp.float32), axis=-1)
    cap = EC_CAPACITY_FACTOR * t // N_EXPERTS
    gates, idx = lax.top_k(aff.T, cap)
    xs = ht[idx]
    a = jnp.einsum('ecd,edf->ecf', xs, w_gate)
    u = jnp.einsum('ecd,edf->ecf', xs, w_up)
    y = jnp.einsum('ecf,efd->ecd', jax.nn.silu(a) * u, w_down) * gates[..., None].astype(h.dtype)
    out = jnp.zeros((t, d), h.dtype).at[idx.reshape(-1)].add(y.reshape(-1, d))
    return out.reshape(b, n, d)

def trunk_layer(x, mod, s_fwd0, s_bwd0, use_rope, norm1_g, norm2_g, w_in, w_fmix, w_out,
                w_router, w_gate, w_up, w_down):
    shift1, scale1, gate1, shift2, scale2, gate2 = jnp.split(mod, 6, axis=-1)
    h = rmsnorm(x, norm1_g) * (1.0 + scale1) + shift1
    p = h @ w_in
    yf = fourier_mix(p[..., :D_FOURIER], w_fmix)
    yr, sf, sb = retention_mixer(p[..., D_FOURIER:], s_fwd0, s_bwd0, use_rope)
    x = x + gate1 * (jnp.concatenate([yf, yr], axis=-1) @ w_out)
    h2 = rmsnorm(x, norm2_g) * (1.0 + scale2) + shift2
    x = x + gate2 * ec_moe(h2, w_router, w_gate, w_up, w_down)
    return x, sf, sb

def setup_inputs(seed: int = 0) -> dict:
    key = jax.random.key(seed)
    ks = jax.random.split(key, 20)
    f32 = jnp.float32
    nrm = lambda k, shape, s: jax.random.normal(k, shape, f32) * s
    return {
        "x_prompt": nrm(ks[0], (BATCH, SEQ, D_MODEL), 1.0),
        "x_sample": nrm(ks[1], (DEC_BATCH, DEC_SEQ, D_MODEL), 1.0),
        "state_ret": nrm(ks[2], (DEC_BATCH, DEPTH, 2, N_RET_HEADS, HEAD_DIM, HEAD_DIM), 0.5),
        "c": nrm(ks[3], (DEC_BATCH, D_MODEL), 1.0),
        "c_ctx": nrm(ks[4], (D_MODEL,), 1.0),
        "norm1_g": 1.0 + nrm(ks[5], (DEPTH, D_MODEL), 0.01),
        "norm2_g": 1.0 + nrm(ks[6], (DEPTH, D_MODEL), 0.01),
        "final_g": 1.0 + nrm(ks[7], (D_MODEL,), 0.01),
        "w_mod": nrm(ks[8], (DEPTH, D_MODEL, 6 * D_MODEL), D_MODEL ** -0.5),
        "b_mod": nrm(ks[9], (DEPTH, 6 * D_MODEL), 0.01),
        "w_in": nrm(ks[10], (DEPTH, D_MODEL, D_IN_PROJ), D_MODEL ** -0.5),
        "w_fmix": nrm(ks[11], (DEPTH, N_FOURIER_GROUPS, FOURIER_GROUP_W, FOURIER_GROUP_W), FOURIER_GROUP_W ** -0.5),
        "w_out": nrm(ks[12], (DEPTH, D_MIX, D_MODEL), D_MIX ** -0.5),
        "w_router": nrm(ks[13], (DEPTH, D_MODEL, N_EXPERTS), D_MODEL ** -0.5),
        "w_gate": nrm(ks[14], (DEPTH, N_EXPERTS, D_MODEL, D_EXPERT_FF), D_MODEL ** -0.5),
        "w_up": nrm(ks[15], (DEPTH, N_EXPERTS, D_MODEL, D_EXPERT_FF), D_MODEL ** -0.5),
        "w_down": nrm(ks[16], (DEPTH, N_EXPERTS, D_EXPERT_FF, D_MODEL), D_EXPERT_FF ** -0.5),
    }

def reference(x_prompt, x_sample, state_ret, c, c_ctx, norm1_g, norm2_g, final_g, w_mod, b_mod,
              w_in, w_fmix, w_out, w_router, w_gate, w_up, w_down):
    xp = x_prompt
    bp = x_prompt.shape[0]
    zeros_s = jnp.zeros((bp, N_RET_HEADS, HEAD_DIM, HEAD_DIM), jnp.float32)
    xs = x_sample
    ctx_states = []
    for l in range(DEPTH):
        mod_ctx = (jax.nn.silu(c_ctx) @ w_mod[l] + b_mod[l])[None, None, :]
        mod_lat = (jax.nn.silu(c) @ w_mod[l] + b_mod[l])[:, None, :]
        xp, sf, sb = trunk_layer(xp, mod_ctx, zeros_s, zeros_s, False, norm1_g[l], norm2_g[l],
                                 w_in[l], w_fmix[l], w_out[l], w_router[l], w_gate[l], w_up[l], w_down[l])
        ctx_states.append(jnp.stack([sf, sb], axis=1))
        s_f0 = state_ret[:, l, 0].astype(jnp.float32)
        s_b0 = state_ret[:, l, 1].astype(jnp.float32)
        xs, _, _ = trunk_layer(xs, mod_lat, s_f0, s_b0, True, norm1_g[l], norm2_g[l],
                               w_in[l], w_fmix[l], w_out[l], w_router[l], w_gate[l], w_up[l], w_down[l])
    y_prompt = rmsnorm(xp, final_g)
    y_sample = rmsnorm(xs, final_g)
    state_ret_new = jnp.stack(ctx_states, axis=1).astype(x_prompt.dtype)
    return (y_prompt, y_sample, state_ret_new)


_drawn_inputs = setup_inputs


def setup_inputs(seed=0):
    import zlib

    import numpy as np

    out = dict(_drawn_inputs(seed))
    spreads = {}
    factors = {'norm1_g': 4.282, 'norm2_g': 4.21, 'final_g': 5.737}
    for name, (base, spread) in spreads.items():
        noise = np.random.default_rng([zlib.crc32(name.encode()), seed]).standard_normal(out[name].shape)
        drawn = base * np.exp(spread * noise) if base else spread * noise
        out[name] = __import__('jax').numpy.asarray(drawn.astype(out[name].dtype))
    for name, factor in factors.items():
        out[name] = (out[name] * factor).astype(out[name].dtype)
    return out
```

```python
import numpy as np
import concourse.bass as bass
from concourse import mybir
from contextlib import ExitStack

F32 = mybir.dt.float32
F32R = mybir.dt.float32r
I32 = mybir.dt.int32
U32 = mybir.dt.uint32
ALU = mybir.AluOpType
ACT = mybir.ActivationFunctionType
AX = mybir.AxisListType

P = 128
D = 1024
NK = D // P
N_S, N_P = 1024, 256
N = N_S + N_P
TS, TP = N_S // P, N_P // P
T = TS + TP
H = 4
DIN = 3072
E = 16
FF = 2816
CS, CP = 2 * N_S // E, 2 * N_P // E
C = CS + CP
W_STEP = 256
STEPS = FF // W_STEP
EPS = 1e-6
SCALE = P ** -0.5


def tables():
    f8, f4 = np.float64, np.float32
    t = {}
    t["c_ident"] = np.eye(P)
    i = np.arange(P, dtype=f8)
    ang = 2 * np.pi * np.outer(i, i) / P
    t["c_chan"] = np.stack([np.cos(ang), -np.sin(ang)], 1) / np.sqrt(P)
    n, k = np.arange(N_S // 2 + 1, dtype=f8), np.arange(N_S // 2 + 1, dtype=f8)
    ang = 2 * np.pi * np.outer(n, k) / N_S
    t["c_poscos"] = np.cos(ang) / np.sqrt(N_S)
    t["c_possin"] = (np.sin(ang) / np.sqrt(N_S))[:N_S // 2, :N_S // 2]
    i2 = np.arange(N_P, dtype=f8)
    ang = 2 * np.pi * np.outer(i2, i2) / N_P
    t["c_ctxdft"] = np.stack([np.cos(ang), np.sin(ang)], 1) / np.sqrt(N_P)
    tok = np.arange(N_S)
    freqs = (f4(10000.0) ** (-np.arange(32, dtype=f4) / f4(32))).astype(f4)
    row = (tok // 64).astype(f4)[:, None] * freqs[None]
    col = (tok % 64).astype(f4)[:, None] * freqs[None]
    full = np.concatenate([row, row, col, col], 1).astype(f8)
    t["c_rope"] = np.stack([np.cos(full), np.sin(full)], 1)
    lg = np.stack([np.log(1.0 - 2.0 ** (-5.0 - np.arange(H))).astype(f4),
                   np.log(1.0 - 2.0 ** (-5.5 - np.arange(H))).astype(f4)], 1).astype(f8)
    j, q = i[:, None], i[None, :]
    mask = np.zeros((P, H, 2, P))
    qdec = np.zeros((P, H, 2, P))
    kdec = np.zeros((P, H, 2))
    for h in range(H):
        mask[:, h, 0] = np.where(q >= j, np.exp(lg[h, 0] * np.maximum(q - j, 0)), 0) * SCALE
        mask[:, h, 1] = np.where(j >= q, np.exp(lg[h, 1] * np.maximum(j - q, 0)), 0) * SCALE
        qdec[:, h, 0] = np.exp(lg[h, 0] * (i + 1))[None]
        qdec[:, h, 1] = np.exp(lg[h, 1] * (P - i))[None]
        kdec[:, h, 0] = np.exp(lg[h, 0] * (P - 1 - i)) * SCALE
        kdec[:, h, 1] = np.exp(lg[h, 1] * i) * SCALE
    t["c_mask"], t["c_qdec"], t["c_kdec"] = mask, qdec, kdec
    t["c_sdec"] = np.broadcast_to(np.exp(lg * P)[None], (P, H, 2))
    return {k: np.ascontiguousarray(v, f4) for k, v in t.items()}


def build(nc, io, stop_after="G"):
    ctx = ExitStack()
    with ctx:
        def sem(name):
            sems.append(nc.alloc_semaphore(name=name))
            return sems[-1]

        sems = []

        def sb(name, shape, dt=F32, c=ctx):
            return c.enter_context(nc.sbuf_tensor(name, shape, dt))

        def ps(name, shape, c, dt=F32):
            return c.enter_context(nc.psum_tensor(name, shape, dt))

        catT = io["catT"] if "catT" in io else nc.dram_tensor("catT", [D, N], F32).ap()
        acc = io["acc"] if "acc" in io else nc.dram_tensor("acc", [N, D], F32).ap()
        xn2 = nc.dram_tensor("xn2", [N, D], F32).ap()

        a_const = sem("a_const")
        ident = sb("ident", [P, P])
        vecT = sb("vecT", [P, 80])
        modT = sb("modT", [P, 6, NK, 2])
        scaleA = sb("scaleA", [P, 2, NK, 2])
        nhalf = sb("nhalf", [P, T])

        def x_rows(t):
            return io["x_sample"][0, t * P:(t + 1) * P, :] if t < TS else io["x_prompt"][0, (t - TS) * P:(t - TS + 1) * P, :]

        def waits(eng, *pairs):
            pairs = [(sm, v if isinstance(v, int) else eng.to_reg(v)) for sm, v in pairs]
            eng.wait_ge(a_const, 16)
            for sm, v in pairs:
                eng.wait_ge(sm, v)

        def req(t):
            return 0 if t < TS else 1

        stack_h = ExitStack()
        hT = [sb("hT_hi", [P, NK, N], F32R, stack_h), sb("hT_lo", [P, NK, N], F32R, stack_h)]
        with ExitStack() as c:
            WR = 2
            vecs = sb("vecs", [80, P], F32, c)
            x = sb("x", [P, T, D], F32, c)
            wm = sb("wm", [P, WR, 6 * D], F32, c)
            cond = sb("cond", [P, NK, 2], F32, c)
            sq = sb("sq", [P, D], F32, c)
            ssum = sb("ssum", [P, T], F32, c)
            rstd = sb("rstd", [P, T], F32, c)
            hfull = sb("hfull", [P, 2, 512], F32, c)
            vps = ps("vps", [P, 80], c)
            mps = ps("mps", [P, 6 * NK, 2], c)
            tps = [ps(f"tps{i}", [P, 512], c) for i in range(3)]
            a_x, a_vec = [sem(f"a_x{i}") for i in range(T)], sem("a_vec")
            a_w = [sem(f"a_w{i}") for i in range(WR)]
            a_vt, a_vtc, a_cond, a_wused, a_mod = sem("a_vt"), sem("a_vtc"), sem("a_cond"), sem("a_wused"), sem("a_mod")
            a_sq, a_mean, a_rstd, a_xn = sem("a_sq"), sem("a_mean"), sem("a_rstd"), sem("a_xn")
            a_scale, a_tp, a_hi, a_full, a_lo = sem("a_scale"), sem("a_tp"), sem("a_hi"), sem("a_full"), sem("a_lo")
            a_half = sem("a_half")
            groups = [(k, g) for k in range(NK) for g in range(3)]

            def group_tiles(g):
                return range(4 * g, min(4 * g + 4, T))

            with nc.Block() as block:
                @block.sync
                def _(sp):
                    sp.dma_start(ident[:], io["c_ident"]).then_inc(a_const, 16)
                    rows = [(io["b_mod"][0].rearrange("(j p) -> j p", p=P), 0, 48),
                            (io["norm1_g"][0].rearrange("(j p) -> j p", p=P), 48, 8),
                            (io["norm2_g"][0].rearrange("(j p) -> j p", p=P), 56, 8),
                            (io["c"][0].rearrange("(j p) -> j p", p=P), 64, 8),
                            (io["c_ctx"].rearrange("(j p) -> j p", p=P), 72, 8)]
                    for src, at, n in rows:
                        sp.dma_start(vecs[at:at + n, :], src).then_inc(a_vec, 16)
                    for k in range(WR):
                        sp.dma_start(wm[:, k, :], io["w_mod"][0, k * P:(k + 1) * P, :]).then_inc(a_w[k], 16)
                    for t in range(T):
                        sp.dma_start(x[:, t, :], x_rows(t)).then_inc(a_x[t], 16)
                    for k in range(WR, NK):
                        sp.wait_ge(a_wused, k - WR + 1)
                        sp.dma_start(wm[:, k % WR, :], io["w_mod"][0, k * P:(k + 1) * P, :]).then_inc(a_w[k % WR], 16)

                @block.tensor
                def _(pe):
                    pe.wait_ge(a_const, 16)
                    pe.wait_ge(a_vec, 5 * 16)
                    pe.transpose(vps[:], vecs[:], ident[0:80, 0:80]).then_inc(a_vt, 1)
                    pe.wait_ge(a_cond, 2)
                    for k in range(NK):
                        pe.wait_ge(a_w[k % WR], 16 * (k // WR + 1))
                        for j in range(6 * NK):
                            mm = pe.matmul(mps[:, j, :], wm[:, k % WR, j * P:(j + 1) * P], cond[:, k, :],
                                           start=(k == 0 and j == 0), stop=(k == NK - 1), skip_group_check=True)
                        mm.then_inc(a_wused, 1)
                    for n, (k, g) in enumerate(groups):
                        if n >= 3:
                            pe.wait_ge(a_full, n - 2)
                        for q, t in enumerate(group_tiles(g)):
                            if k == 0:
                                pe.wait_ge(a_xn, t + 1)
                            mm = pe.transpose(tps[n % 3][:, q * P:(q + 1) * P], x[:, t, k * P:(k + 1) * P], ident[:])
                        mm.then_inc(a_tp, 1)

                @block.scalar
                def _(act):
                    act.wait_ge(a_vtc, 1)
                    act.activation(cond[:, :, 0], vecT[:, 64:72], ACT.Silu).then_inc(a_cond, 1)
                    act.activation(cond[:, :, 1], vecT[:, 72:80], ACT.Silu).then_inc(a_cond, 1)
                    for t in range(T):
                        act.wait_ge(a_x[t], 16)
                        if t:
                            act.wait_ge(a_sq, t)
                        act.activation(sq[:], x[:, t, :], ACT.Square, accum_out=ssum[:, t:t + 1]).then_inc(a_sq, 1)
                    for n, (k, g) in enumerate(groups):
                        a, b = 512 * g, min(512 * g + 512, N)
                        act.wait_ge(a_full, n + 1)
                        act.activation(hT[0][:, k, a:b], hfull[:, n % 2, 0:b - a], ACT.Copy).then_inc(a_hi, 1)

                @block.gpsimd
                def _(gp):
                    gp.memset(nhalf[:], -0.5).then_inc(a_half, 1)
                    gp.wait_ge(a_sq, T)
                    gp.tensor_scalar(ssum[:], ssum[:], 1.0 / D, EPS, ALU.mult, ALU.add).then_inc(a_mean, 1)
                    gp.wait_ge(a_mean, 1)
                    gp.wait_ge(a_half, 1)
                    gp.tensor_tensor(rstd[:], ssum[:], nhalf[:], ALU.pow).then_inc(a_rstd, 1)
                    for n, (k, g) in enumerate(groups):
                        a, b = 512 * g, min(512 * g + 512, N)
                        gp.wait_ge(a_hi, n + 1)
                        gp.tensor_tensor(hT[1][:, k, a:b], hfull[:, n % 2, 0:b - a], hT[0][:, k, a:b].bitcast(F32),
                                         ALU.subtract).then_inc(a_lo, 1)

                @block.vector
                def _(dve):
                    dve.wait_ge(a_vt, 1)
                    dve.tensor_copy(vecT[:], vps[:]).then_inc(a_vtc, 1)
                    dve.wait_ge(a_rstd, 1)
                    for t in range(T):
                        dve.tensor_scalar(x[:, t, :], x[:, t, :], rstd[:, t:t + 1], None, ALU.mult).then_inc(a_xn, 1)
                    dve.wait_ge(a_wused, NK)
                    dve.wait_ge(a_vtc, 1)
                    bm = vecT[:, 0:48].unsqueeze(2).broadcast_to([P, 48, 2])
                    dve.tensor_tensor(modT[:].rearrange("p a k r -> p (a k) r"), mps[:], bm, ALU.add).then_inc(a_mod, 1)
                    dve.wait_ge(a_mod, 1)
                    for m in range(2):
                        gm = vecT[:, 48 + 8 * m:56 + 8 * m].unsqueeze(2).broadcast_to([P, NK, 2])
                        dve.scalar_tensor_tensor(scaleA[:, m, :, :], modT[:, 1 + 3 * m, :, :], 1.0, gm,
                                                 ALU.add, ALU.mult).then_inc(a_scale, 1)
                    dve.wait_ge(a_scale, 2)
                    for n, (k, g) in enumerate(groups):
                        a, b = 512 * g, min(512 * g + 512, N)
                        r = 0 if g < 2 else 1
                        dve.wait_ge(a_tp, n + 1)
                        if n >= 2:
                            dve.wait_ge(a_lo, n - 1)
                        dve.tensor_scalar(hfull[:, n % 2, 0:b - a], tps[n % 3][:, 0:b - a],
                                          scaleA[:, 0, k, r:r + 1], modT[:, 0, k, r:r + 1],
                                          ALU.mult, ALU.add).then_inc(a_full, 1)

        with ExitStack() as c:
            NG = 4
            raw = sb("raw", [P, NG, 384], F32, c)
            wq = [sb("wq_hi", [P, NK, 384], F32R, c), sb("wq_lo", [P, NK, 384], F32R, c)]
            wg = [sb("wg_hi", [P, NK, 256], F32R, c), sb("wg_lo", [P, NK, 256], F32R, c)]
            p = sb("p", [P, T, 384], F32, c)
            AT = sb("AT", [P, T, 2, P], F32, c)
            qTd = sb("qTd", [P, T, 2, P], F32, c)
            S = sb("S", [P, T, 2, P], F32, c)
            rope = sb("rope", [P, TS, 2, P], F32, c)
            mask = sb("mask", [P, H, 2, P], F32, c)
            qdec = sb("qdec", [P, H, 2, P], F32, c)
            kdec = sb("kdec", [P, H, 2], F32, c)
            sdec = sb("sdec", [P, H, 2], F32, c)
            rt = sb("rt", [P, 2, 2, P], F32, c)
            qkT = sb("qkT", [P, 2, 2, P], F32, c)
            vdec = sb("vdec", [P, 2, 2, P], F32, c)
            fin = sb("fin", [P, 2, P], F32, c)
            stats = sb("stats", [P, 2, 2, 6], F32, c)
            mv = sb("mv", [P, 2, 2, 2], F32, c)
            var = sb("var", [P, 2, 2], F32, c)
            rs = sb("rs", [P, 2, 2], F32, c)
            z = sb("z", [P, 2, 2, P], F32, c)
            ysb = sb("ysb", [P, 2, P], F32, c)
            yT = sb("yT", [P, 2, P], F32, c)
            proj = [ps(f"proj{i}", [P, 512], c) for i in range(2)]
            tp = ps("tp", [P, 512], c)
            att = ps("att", [P, 512], c)
            ups = ps("ups", [P, 512], c)
            ops = [ps(f"ops{i}", [P, 512], c) for i in range(2)]
            yps = ps("yps", [P, 512], c)
            b_tab = sem("b_tab")
            b_raw = [sem(f"b_raw{i}") for i in range(NG)]
            b_hi, b_lo = sem("b_hi"), sem("b_lo")
            b_proj = sem("b_proj")
            b_qkv = sem("b_qkv")
            b_rt, b_rope = sem("b_rt"), sem("b_rope")
            b_vdec, b_gate = sem("b_vdec"), sem("b_gate")
            b_tr, b_trc, b_qtd = sem("b_tr"), sem("b_trc"), sem("b_qtd")
            b_att, b_atm = sem("b_att"), sem("b_atm")
            b_u, b_ud = sem("b_u"), sem("b_ud")
            b_s0, b_sb, b_fin, b_finout = sem("b_s0"), sem("b_sb"), sem("b_fin"), sem("b_finout")
            b_o, b_st, b_mv, b_var, b_rs = sem("b_o"), sem("b_st"), sem("b_mv"), sem("b_var"), sem("b_rs")
            b_z, b_zg, b_y = sem("b_z"), sem("b_zg"), sem("b_y")
            b_yt, b_yc = sem("b_yt"), sem("b_yc")
            b_yout = [sem("b_yout0"), sem("b_yout1")]

            w_in = io["w_in"][0].rearrange("(k p) (s c) -> k p s c", p=P, s=6)
            nc.clear_and_free_semaphores([sm for sm in sems if sm.name.startswith("a_") and sm not in (a_const, *a_x)])
            state_in, state_out = io["state_ret"], io["state_out"]
            ORDER = [9, 8] + list(range(TS - 1, -1, -1))

            def heads(eng, body):
                with eng.Fori(0, H - 1) as h:
                    body(h, False)
                body(H - 1, True)

            with nc.Block() as block:
                @block.sync
                def _(sp):
                    for dst, src in ((mask, "c_mask"), (qdec, "c_qdec"), (kdec, "c_kdec"), (sdec, "c_sdec")):
                        sp.dma_start(dst[:], io[src]).then_inc(b_tab, 16)
                    sp.dma_start(rope[:], io["c_rope"].rearrange("(t p) a c -> p t a c", p=P)).then_inc(b_tab, 16)
                    for sm in b_yout:
                        sp.sem_inc(sm, 16)
                    sp.sem_inc(b_finout, 32)

                    def row_tile(h, k, gates, use):
                        lo, hi = (4, 6) if gates else (1, 4)
                        sp.wait_ge(b_hi, use + 1)
                        sp.wait_ge(b_lo, use + 1)
                        dst = raw[:, k % NG, 0:P * (hi - lo)].rearrange("p (s c) -> p s c", c=P)
                        sp.dma_start(dst, w_in[k, :, lo:hi, bass.ds(h * P, P)]).then_inc(b_raw[k % NG], 16)

                    def first_states(h):
                        for d, at in ((0, 0), (1, TS - 1)):
                            src = state_in[0, 0, d, bass.ds(h, 1), :, :].rearrange("a p e -> p (a e)")
                            sp.dma_start(S[:, at, d, :], src).then_inc(b_s0, 16)

                    for k in range(NK):
                        row_tile(0, k, False, k)
                    first_states(0)

                    def body(h, last):
                        for k in range(NK):
                            row_tile(h, k, True, NK + 2 * NK * h + k)
                        for g in range(T + 4):
                            if g < NK and not last:
                                row_tile(h + 1, g, False, 2 * NK * (h + 1) + g)
                            if g == 4:
                                sp.wait_ge(b_fin, h + 1)
                                for d in range(2):
                                    dst = state_out[0, 0, d, bass.ds(h, 1), :, :].rearrange("a p e -> p (a e)")
                                    sp.dma_start(dst, fin[:, d, :]).then_inc(b_finout, 16)
                            if g >= 4:
                                j = g - 4
                                t = ORDER[j]
                                waits(sp, (b_yc, 1 + T * h + j + 1))
                                dst = catT[bass.ds((H + h) * P, P), t * P:(t + 1) * P]
                                sp.dma_start(dst, yT[:, j % 2, :]).then_inc(b_yout[j % 2], 16)
                        if not last:
                            sp.wait_ge(b_o, T * (h + 1))
                            first_states(h + 1)

                    heads(sp, body)
                    for sm in b_yout:
                        sp.wait_ge(sm, 16 + 16 * H * T // 2)
                    sp.wait_ge(b_finout, 32 + 32 * H)

                @block.tensor
                def _(pe):
                    pe.wait_ge(a_const, 16)
                    for sm, n in ((b_att, 2), (b_u, 2), (b_yt, 2)):
                        pe.sem_inc(sm, n)

                    def project(t, use, w, cols):
                        for k in range(NK):
                            for a, b in ((0, 0), (0, 1), (1, 0)):
                                mm = pe.matmul(proj[use % 2][:, 0:cols], hT[a][:, k, t * P:(t + 1) * P], w[b][:, k, :],
                                               start=(k == 0 and a == b), stop=(k == NK - 1 and a == 1))
                        mm.then_inc(b_proj, 1)

                    def body(h, last):
                        for s in range(T + 2):
                            if s < T:
                                if s == 0:
                                    pe.wait_ge(b_hi, NG + 2 * NK * h + NK)
                                    pe.wait_ge(b_lo, NG + 2 * NK * h + NK)
                                if s >= 2:
                                    pe.wait_ge(b_qkv, T * h + s - 1)
                                else:
                                    pe.wait_ge(b_gate, T * h + s + 1)
                                project(s, s, wq, 384)
                            if 1 <= s <= T:
                                t = s - 1
                                if t < TS:
                                    pe.wait_ge(b_rope, 1 + TS * h + t + 1)
                                else:
                                    pe.wait_ge(b_qkv, T * h + t + 1)
                                pe.wait_ge(b_trc, T * h + t + 1)
                                pe.transpose(tp[:, 0:P], p[:, t, 0:P], ident[:])
                                pe.transpose(tp[:, P:2 * P], p[:, t, P:2 * P], ident[:]).then_inc(b_tr, 1)
                                pe.wait_ge(b_vdec, T * h + t + 1)
                                pe.wait_ge(b_ud, T * h + t + 1)
                                pe.matmul(ups[:, 0:2 * P], p[:, t, P:2 * P], vdec[:, t % 2, :, :],
                                          start=True, stop=True).then_inc(b_u, 1)
                            if s >= 2:
                                t = s - 2
                                pe.wait_ge(b_trc, 1 + T * h + t + 1)
                                pe.wait_ge(b_atm, T * h + t + 1)
                                pe.matmul(att[:, 0:P], qkT[:, t % 2, 1, :], qkT[:, t % 2, 0, :],
                                          start=True, stop=True).then_inc(b_att, 1)
                        for g in range(T + 3):
                            if g < T:
                                if g == 0:
                                    pe.wait_ge(b_hi, NG + 2 * NK * h + 2 * NK)
                                    pe.wait_ge(b_lo, NG + 2 * NK * h + 2 * NK)
                                if g < 2:
                                    pe.wait_ge(b_qkv, T * h + T - 1 + g)
                                else:
                                    pe.wait_ge(b_gate, 2 + T * h + g - 1)
                                project(ORDER[g], g, wg, 256)
                                t = ORDER[g]
                                if g == 0:
                                    pe.wait_ge(b_atm, 1 + T * h + T)
                                    pe.wait_ge(b_qtd, 2 + T * h + T)
                                    pe.wait_ge(b_ud, 1 + T * h + T)
                                if t < TS - 1:
                                    pe.wait_ge(b_sb, (TS - 1) * h + TS - 1 - t)
                                pe.wait_ge(b_z, T * h + g + 1)
                                for d in range(2):
                                    alone = (t, d) in ((TS, 0), (T - 1, 1))
                                    mm = pe.matmul(ops[g % 2][:, d * P:(d + 1) * P], AT[:, t, d, :],
                                                   p[:, t, 2 * P:3 * P], start=True, stop=alone)
                                    if not alone:
                                        mm = pe.matmul(ops[g % 2][:, d * P:(d + 1) * P], qTd[:, t, d, :],
                                                       S[:, t, d, :], start=False, stop=True)
                                mm.then_inc(b_o, 1)
                            if g >= 3:
                                j = g - 3
                                pe.wait_ge(b_y, 2 + T * h + j + 1)
                                pe.wait_ge(b_yc, T * h + j + 1)
                                pe.transpose(yps[:, 0:P], ysb[:, j % 2, :], ident[:]).then_inc(b_yt, 1)

                    heads(pe, body)

                @block.scalar
                def _(act):
                    for sm, n in ((b_hi, NG), (b_gate, 2), (b_trc, 1), (b_yc, 1)):
                        act.sem_inc(sm, n)

                    def split_hi(h, k, gates):
                        act.wait_ge(b_raw[k % NG], 16 * (4 * h + (2 if gates else 0) + k // NG + 1))
                        dst, cols = (wg[0], 256) if gates else (wq[0], 384)
                        act.activation(dst[:, k, :], raw[:, k % NG, 0:cols], ACT.Copy).then_inc(b_hi, 1)

                    for k in range(NK):
                        split_hi(0, k, False)
                    act.wait_ge(b_tab, 5 * 16)

                    def body(h, last):
                        for s in range(T + 1):
                            if s < T:
                                act.wait_ge(b_proj, 2 * T * h + s + 1)
                                act.activation(p[:, s, :], proj[s % 2][:, 0:3 * P], ACT.Copy).then_inc(b_qkv, 1)
                                waits(act, (b_qkv, T * h + s + 1), (b_u, T * h + s + 1))
                                for d in range(2):
                                    op = act.activation(vdec[:, s % 2, d, :], p[:, s, 2 * P:3 * P], ACT.Copy,
                                                        scale=kdec[:, bass.ds(h, 1), d])
                                op.then_inc(b_vdec, 1)
                            if s < NK:
                                split_hi(h, s, True)
                            if s >= 1:
                                t = s - 1
                                act.wait_ge(b_tr, T * h + t + 1)
                                act.wait_ge(b_att, T * h + t + 1)
                                act.wait_ge(b_qtd, T * h + t + 1)
                                act.activation(qkT[:, t % 2, :, :].rearrange("p a c -> p (a c)"), tp[:, 0:2 * P],
                                               ACT.Copy).then_inc(b_trc, 1)
                        for g in range(T + 3):
                            if g < T:
                                act.wait_ge(b_proj, 2 * T * h + T + g + 1)
                                act.wait_ge(b_zg, T * h + g + 1)
                                act.activation(p[:, ORDER[g], 0:2 * P], proj[g % 2][:, 0:2 * P],
                                               ACT.Silu).then_inc(b_gate, 1)
                            if g < NK and not last:
                                split_hi(h + 1, g, False)
                            if g >= 3:
                                j = g - 3
                                act.wait_ge(b_yt, 2 + T * h + j + 1)
                                act.wait_ge(b_yout[j % 2], 16 * (T // 2 * h + j // 2 + 1))
                                act.activation(yT[:, j % 2, :], yps[:, 0:P], ACT.Copy).then_inc(b_yc, 1)

                    heads(act, body)

                @block.vector
                def _(dve):
                    for sm, n in ((b_lo, NG), (b_ud, 1), (b_atm, 1), (b_z, 2)):
                        dve.sem_inc(sm, n)

                    def split_lo(h, k, gates):
                        dve.wait_ge(b_hi, NG + 2 * NK * h + (NK if gates else 0) + k + 1)
                        (w_hi, w_lo), cols = (wg, 256) if gates else (wq, 384)
                        dve.tensor_tensor(w_lo[:, k, :], raw[:, k % NG, 0:cols], w_hi[:, k, :].bitcast(F32),
                                          ALU.subtract).then_inc(b_lo, 1)

                    for k in range(NK):
                        split_lo(0, k, False)
                    dve.wait_ge(b_tab, 5 * 16)

                    def body(h, last):
                        sd = [sdec[:, bass.ds(h, 1), d] for d in range(2)]
                        for s in range(T + 2):
                            if s < TS:
                                dve.wait_ge(b_qkv, T * h + s + 1)
                                dve.wait_ge(b_rope, TS * h + s + 1)
                                qk = p[:, s, 0:2 * P].rearrange("p (z c) -> p z c", z=2)
                                for a in range(2):
                                    tab = rope[:, s, a, :].unsqueeze(1).broadcast_to([P, 2, P])
                                    op = dve.tensor_tensor(rt[:, a, :, :], qk, tab, ALU.mult)
                                op.then_inc(b_rt, 1)
                            if s < NK:
                                split_lo(h, s, True)
                            if 1 <= s <= T:
                                t = s - 1
                                dve.wait_ge(b_u, 2 + T * h + t + 1)
                                dve.wait_ge(b_ud, 1 + T * h + t)
                                if t == 0:
                                    dve.wait_ge(b_s0, 32 * h + 32)
                                uf, ub = ups[:, 0:P], ups[:, P:2 * P]
                                if t < TS - 1:
                                    op = dve.scalar_tensor_tensor(S[:, t + 1, 0, :], S[:, t, 0, :], sd[0], uf,
                                                                  ALU.mult, ALU.add)
                                if 1 <= t < TS:
                                    op = dve.tensor_copy(S[:, t - 1, 1, :], ub)
                                if t == TS:
                                    dve.tensor_copy(S[:, t + 1, 0, :], uf)
                                    dve.wait_ge(b_finout, 32 * h + 32)
                                    op = dve.tensor_copy(fin[:, 1, :], ub)
                                if t == TS + 1:
                                    dve.scalar_tensor_tensor(fin[:, 0, :], S[:, t, 0, :], sd[0], uf, ALU.mult, ALU.add)
                                    dve.scalar_tensor_tensor(fin[:, 1, :], ub, sd[1], fin[:, 1, :],
                                                             ALU.mult, ALU.add).then_inc(b_fin, 1)
                                    op = dve.tensor_copy(S[:, t - 1, 1, :], ub)
                                op.then_inc(b_ud, 1)
                            if s >= 2:
                                t = s - 2
                                dve.wait_ge(b_att, 2 + T * h + t + 1)
                                m = mask[:, bass.ds(h, 1), :, :].rearrange("p a d c -> p (a d) c")
                                dve.tensor_tensor(AT[:, t, :, :], att[:, 0:P].unsqueeze(1).broadcast_to([P, 2, P]), m,
                                                  ALU.mult).then_inc(b_atm, 1)
                        dve.wait_ge(b_ud, 1 + T * h + T)
                        for n in range(TS - 1):
                            t = TS - 1 - n
                            if n:
                                dve.wait_ge(b_sb, (TS - 1) * h + n)
                            dve.scalar_tensor_tensor(S[:, t - 1, 1, :], S[:, t, 1, :], sd[1], S[:, t - 1, 1, :],
                                                     ALU.mult, ALU.add).then_inc(b_sb, 1)
                        for j in range(T + 1):
                            if j < T:
                                dve.wait_ge(b_o, T * h + j + 1)
                                for d in range(2):
                                    op = dve.bn_stats(stats[:, j % 2, d, :], ops[j % 2][:, d * P:(d + 1) * P])
                                op.then_inc(b_st, 1)
                                waits(dve, (b_st, T * h + j + 1))
                                for d in range(2):
                                    op = dve.bn_aggr(mv[:, j % 2, d, :], stats[:, j % 2, d, :])
                                op.then_inc(b_mv, 1)
                            if j < NK and not last:
                                split_lo(h + 1, j, False)
                            if j >= 1:
                                i = j - 1
                                dve.wait_ge(b_rs, T * h + i + 1)
                                dve.wait_ge(b_y, T * h + i + 1)
                                for d in range(2):
                                    op = dve.tensor_scalar(z[:, i % 2, d, :], ops[i % 2][:, d * P:(d + 1) * P],
                                                           mv[:, i % 2, d, 0:1], rs[:, i % 2, d:d + 1],
                                                           ALU.subtract, ALU.mult)
                                op.then_inc(b_z, 1)

                    heads(dve, body)

                @block.gpsimd
                def _(gp):
                    for sm, n in ((b_rope, 1), (b_qtd, 2), (b_zg, T), (b_y, 2)):
                        gp.sem_inc(sm, n)
                    gp.wait_ge(b_tab, 5 * 16)

                    def body(h, last):
                        for s in range(T + 1):
                            if s < TS:
                                gp.wait_ge(b_rt, TS * h + s + 1)
                                cs = rt[:, 0, :, :].rearrange("p z (a s w) -> p (z a) s w", a=2, s=2)
                                sn = rt[:, 1, :, :].rearrange("p z (a s w) -> p (z a) s w", a=2, s=2)
                                out = p[:, s, 0:2 * P].rearrange("p (z s w) -> p z s w", s=2, w=32)
                                gp.tensor_tensor(out[:, :, 0, :], cs[:, :, 0, :], sn[:, :, 1, :], ALU.subtract)
                                gp.tensor_tensor(out[:, :, 1, :], cs[:, :, 1, :], sn[:, :, 0, :],
                                                 ALU.add).then_inc(b_rope, 1)
                            if s >= 1:
                                t = s - 1
                                waits(gp, (b_trc, 1 + T * h + t + 1))
                                qd = qdec[:, bass.ds(h, 1), :, :].rearrange("p a d c -> p (a d) c")
                                gp.tensor_tensor(qTd[:, t, :, :], qkT[:, t % 2, 0, :].unsqueeze(1).broadcast_to([P, 2, P]),
                                                 qd, ALU.mult).then_inc(b_qtd, 1)
                        for j in range(T + 1):
                            if j < T:
                                waits(gp, (b_mv, T * h + j + 1))
                                gp.tensor_scalar(var[:, j % 2, :], mv[:, j % 2, :, 1], EPS, None, ALU.add).then_inc(b_var, 1)
                                gp.wait_ge(b_var, T * h + j + 1)
                                gp.tensor_tensor(rs[:, j % 2, :], var[:, j % 2, :], nhalf[:, 0:2], ALU.pow).then_inc(b_rs, 1)
                            if j >= 1:
                                i = j - 1
                                gp.wait_ge(b_z, 2 + T * h + i + 1)
                                gp.wait_ge(b_gate, 2 + T * h + i + 1)
                                zi = z[:, i % 2, :, :].rearrange("p d c -> p (d c)")
                                gp.tensor_tensor(zi, zi, p[:, ORDER[i], 0:2 * P], ALU.mult).then_inc(b_zg, 1)
                                gp.wait_ge(b_zg, T + T * h + i + 1)
                                gp.wait_ge(b_yt, T * h + i + 1)
                                gp.tensor_tensor(ysb[:, i % 2, :], z[:, i % 2, 0, :], z[:, i % 2, 1, :],
                                                 ALU.add).then_inc(b_y, 1)

                    heads(gp, body)

        with ExitStack() as c:
            NG = 4
            raw = sb("rawC", [P, NG, P], F32, c)
            w = [sb("wf_hi", [P, NK, P], F32R, c), sb("wf_lo", [P, NK, P], F32R, c)]
            chan = sb("chan", [P, 2, P], F32, c)
            wmix = sb("wmix", [P, H, P], F32, c)
            M = sb("M", [P, H, 2, P], F32, c)
            pcos = sb("pcos", [P, 4, 513], F32, c)
            palt = sb("palt", [1, 513], F32, c)
            psin = sb("psin", [P, 4, 512], F32, c)
            cdft = sb("cdft", [P, 2, 2, N_P], F32, c)
            UT = sb("UT", [P, N], F32, c)
            Ue = sb("Ue", [P, 513], F32, c)
            Uo = sb("Uo", [P, 512], F32, c)
            Z = sb("Z", [P, 6, 2, P], F32, c)
            Zrow = sb("Zrow", [1, P], F32, c)
            Bs = sb("Bs", [P, 512], F32, c)
            yf = sb("yf", [P, N], F32, c)
            up = [ps(f"up{i}", [P, 512], c) for i in range(3)]
            zp = [ps(f"zp{i}", [P, 512], c) for i in range(2)]
            pa, pb, pm = ps("pa", [P, 512], c), ps("pb", [P, 512], c), ps("pm", [P, 512], c)
            c_tab, c_raw = sem("c_tab"), [sem(f"c_raw{i}") for i in range(NG)]
            c_hi, c_lo, c_m, c_mc = sem("c_hi"), sem("c_lo"), sem("c_m"), sem("c_mc")
            c_up, c_ut = sem("c_up"), sem("c_ut")
            c_fold, c_z, c_za, c_zd = sem("c_fold"), sem("c_z"), sem("c_za"), sem("c_zd")
            c_row, c_rowc = sem("c_row"), sem("c_rowc")
            c_pos, c_bs, c_yd, c_ya, c_out = sem("c_pos"), sem("c_bs"), sem("c_yd"), sem("c_ya"), sem("c_out")
            w_in = io["w_in"][0].rearrange("(k p) c -> k p c", p=P)
            token_groups = [(0, 512), (512, 1024), (1024, 1280)]

            with nc.Block() as block:
                @block.sync
                def _(sp):
                    sp.dma_start(chan[:], io["c_chan"]).then_inc(c_tab, 16)
                    sp.dma_start(wmix[:], io["w_fmix"][0].rearrange("g w v -> w g v")).then_inc(c_tab, 16)
                    sp.sem_inc(c_out, 16)

                    def weights(g):
                        for k in range(NK):
                            sp.wait_ge(c_hi, NK * g + k + 1)
                            sp.wait_ge(c_lo, NK * g + k + 1)
                            sp.dma_start(raw[:, k % NG, :], w_in[k, :, bass.ds(g * P, P)]).then_inc(c_raw[k % NG], 16)

                    def store(g):
                        sp.wait_ge(c_yd, 1 + g + 1)
                        sp.wait_ge(c_ya, 1 + g + 1)
                        sp.dma_start(catT[bass.ds(g * P, P), :], yf[:]).then_inc(c_out, 16)

                    weights(0)
                    sp.dma_start(pcos[:], io["c_poscos"][0:512, :].rearrange("(t p) k -> p t k", p=P)).then_inc(c_tab, 16)
                    sp.dma_start(palt[:], io["c_poscos"][512:513, :]).then_inc(c_tab, 16)
                    sp.dma_start(psin[:], io["c_possin"].rearrange("(t p) k -> p t k", p=P)).then_inc(c_tab, 16)
                    sp.dma_start(cdft[:], io["c_ctxdft"].rearrange("(t p) a k -> p t a k", p=P)).then_inc(c_tab, 16)
                    with sp.Fori(0, H - 1) as g:
                        weights(g + 1)
                        store(g)
                    store(H - 1)
                    sp.wait_ge(c_out, 16 + 16 * H)

                @block.tensor
                def _(pe):
                    def project(g):
                        pe.wait_ge(c_hi, NG + NK * g + NK)
                        pe.wait_ge(c_lo, NG + NK * g + NK)
                        for q, (a, b) in enumerate(token_groups):
                            pe.wait_ge(c_ut, 3 * g + q + 1)
                            for k in range(NK):
                                for i, j in ((0, 0), (0, 1), (1, 0)):
                                    mm = pe.matmul(up[q][:, 0:b - a], w[i][:, k, :], hT[j][:, k, a:b],
                                                   start=(k == 0 and i == j), stop=(k == NK - 1 and i == 1))
                            mm.then_inc(c_up, 1)

                    def mix(g):
                        m = M[:, bass.ds(g, 1), :, :].rearrange("p g a v -> p (g a) v")
                        pe.wait_ge(c_fold, g + 1)
                        for n in range(6):
                            pe.wait_ge((c_za, c_zd)[n % 2], 3 * g + n // 2 + 1)
                            if n < 4:
                                pe.matmul(zp[n % 2][:, 0:P], Ue[:, n * P:(n + 1) * P], m[:, 0, :], start=True, stop=True)
                                mm = pe.matmul(zp[n % 2][:, P:2 * P], Uo[:, n * P:(n + 1) * P], m[:, 1, :],
                                               start=True, stop=True)
                            else:
                                t = TS + n - 4
                                mm = pe.matmul(zp[n % 2][:, 0:2 * P], UT[:, t * P:(t + 1) * P], m, start=True, stop=True)
                            mm.then_inc(c_z, 1)
                            if n == 3:
                                waits(pe, (c_yd, g + 1), (c_ya, g + 1))
                                pe.matmul(pm[0:1, 384:512], Ue[:, 512:513], m[:, 0, :], start=True,
                                          stop=True).then_inc(c_row, 1)
                        for n in range(4):
                            pe.wait_ge((c_za, c_zd)[n % 2], 1 + 3 * g + n // 2 + 1)
                            pe.matmul(pa[:], Z[:, n, 0, :], pcos[:, n, 0:512], start=(n == 0), stop=False)
                            pe.matmul(pb[:], Z[:, n, 1, :], psin[:, n, :], start=(n == 0), stop=(n == 3))
                        pe.wait_ge(c_rowc, g + 1)
                        pe.matmul(pa[:], Zrow[:], palt[:, 0:512], start=False, stop=True)
                        for n in range(4):
                            pe.matmul(pm[:, 256:257], Z[:, n, 0, :], pcos[:, n, 512:513], start=(n == 0), stop=False)
                        pe.matmul(pm[:, 256:257], Zrow[:], palt[:, 512:513], start=False, stop=True)
                        pe.wait_ge(c_za, 1 + 3 * g + 3)
                        pe.wait_ge(c_zd, 1 + 3 * g + 3)
                        for n in range(2):
                            for a in range(2):
                                mm = pe.matmul(pm[:, 0:N_P], Z[:, 4 + n, a, :], cdft[:, n, a, :],
                                               start=(n + a == 0), stop=(n + a == 2))
                        mm.then_inc(c_pos, 1)

                    pe.wait_ge(c_tab, 6 * 16)
                    for g in range(H):
                        for a in range(2):
                            mm = pe.matmul(zp[g // 2][:, (g % 2 * 2 + a) * P:(g % 2 * 2 + a + 1) * P], chan[:, a, :],
                                           wmix[:, g, :], start=True, stop=True)
                        mm.then_inc(c_m, 1)
                    project(0)
                    pe.wait_ge(c_mc, 2)
                    with pe.Fori(0, H - 1) as g:
                        project(g + 1)
                        mix(g)
                    mix(H - 1)

                def copy_z(eng, fn, g, n, done):
                    eng.wait_ge(c_z, 6 * g + n + 1)
                    fn(Z[:, n, :, :].rearrange("p a v -> p (a v)"), zp[n % 2][:, 0:2 * P]).then_inc(done, 1)

                @block.scalar
                def _(act):
                    for sm, n in ((c_hi, NG), (c_ut, 3), (c_za, 1), (c_ya, 1)):
                        act.sem_inc(sm, n)

                    def split_hi(g):
                        for k in range(NK):
                            act.wait_ge(c_raw[k % NG], 16 * (2 * g + k // NG + 1))
                            if k == 0 and not isinstance(g, int):
                                act.wait_ge(c_up, 3 * g)
                            act.activation(w[0][:, k, :], raw[:, k % NG, :], ACT.Copy).then_inc(c_hi, 1)

                    def take_u(g):
                        for q, (a, b) in enumerate(token_groups):
                            act.wait_ge(c_up, 3 * g + q + 1)
                            act.activation(UT[:, a:b], up[q][:, 0:b - a], ACT.Copy).then_inc(c_ut, 1)

                    def tiles(g):
                        for n in (0, 2, 4):
                            copy_z(act, lambda o, i: act.activation(o, i, ACT.Copy), g, n, c_za)
                            if n == 2:
                                act.wait_ge(c_row, g + 1)
                                act.activation(Zrow[:], pm[0:1, 384:512], ACT.Copy).then_inc(c_rowc, 1)

                    def finish(g):
                        act.wait_ge(c_pos, g + 1)
                        act.activation(Bs[:], pb[:], ACT.Copy).then_inc(c_bs, 1)
                        act.wait_ge(c_out, 16 * (g + 1))
                        act.activation(yf[:, 512:513], pm[:, 256:257], ACT.Copy)
                        act.activation(yf[:, N_S:N], pm[:, 0:N_P], ACT.Copy).then_inc(c_ya, 1)

                    split_hi(0)
                    for i in range(2):
                        act.wait_ge(c_m, 2 * i + 2)
                        act.activation(M[:, 2 * i:2 * i + 2, :, :].rearrange("p g a v -> p (g a v)"), zp[i][:],
                                       ACT.Copy).then_inc(c_mc, 1)
                    take_u(0)
                    with act.Fori(0, H - 1) as g:
                        split_hi(g + 1)
                        tiles(g)
                        act.wait_ge(c_fold, g + 1)
                        act.wait_ge(c_z, 6 * g + 6)
                        take_u(g + 1)
                        finish(g)
                    tiles(H - 1)
                    finish(H - 1)

                @block.vector
                def _(dve):
                    for sm, n in ((c_lo, NG), (c_zd, 1), (c_yd, 1)):
                        dve.sem_inc(sm, n)

                    def split_lo(g):
                        for k in range(NK):
                            dve.wait_ge(c_hi, NG + NK * g + k + 1)
                            dve.tensor_tensor(w[1][:, k, :], raw[:, k % NG, :], w[0][:, k, :].bitcast(F32),
                                              ALU.subtract).then_inc(c_lo, 1)

                    def fold(g):
                        dve.wait_ge(c_ut, 3 + 3 * g + 2)
                        back = UT[:, 1023:512:-1]
                        dve.tensor_tensor(Ue[:, 1:512], UT[:, 1:512], back, ALU.add)
                        dve.tensor_tensor(Uo[:, 1:512], UT[:, 1:512], back, ALU.subtract)
                        dve.tensor_copy(Ue[:, 0:513:512], UT[:, 0:513:512]).then_inc(c_fold, 1)

                    def tiles(g):
                        for n in (1, 3, 5):
                            copy_z(dve, dve.tensor_copy, g, n, c_zd)

                    def finish(g):
                        dve.wait_ge(c_bs, g + 1)
                        dve.wait_ge(c_out, 16 * (g + 1))
                        dve.tensor_tensor(yf[:, 0:512], pa[:], Bs[:], ALU.add)
                        dve.tensor_tensor(yf[:, 1023:512:-1], pa[:, 1:512], Bs[:, 1:512], ALU.subtract).then_inc(c_yd, 1)

                    dve.memset(Uo[:, 0:1], 0.0)
                    split_lo(0)
                    fold(0)
                    with dve.Fori(0, H - 1) as g:
                        split_lo(g + 1)
                        tiles(g)
                        dve.wait_ge(c_row, g + 1)
                        fold(g + 1)
                        finish(g)
                    tiles(H - 1)
                    finish(H - 1)
        stack_h.close()

        if stop_after == "C":
            return

        L = sb("L", [P, T, E])
        gates = [sb("gate1", [P, 2, D]), sb("gate2", [P, 2, D])]
        with ExitStack() as c:
            NW = 2
            rawo = sb("rawo", [P, NW, D], F32, c)
            wo = [sb("wo_hi", [P, NK, D], F32R, c), sb("wo_lo", [P, NK, D], F32R, c)]
            ones = sb("ones", [P, P], F32, c)
            diag = sb("diag", [P, 2, P], F32, c)
            rawc = sb("rawc", [P, 2, NK, P], F32, c)
            ca = [sb("cat_hi", [P, 2, NK, P], F32R, c), sb("cat_lo", [P, 2, NK, P], F32R, c)]
            xt = sb("xt", [P, 2, D], F32, c)
            x1 = sb("x1", [P, 2, D], F32, c)
            xn = sb("xn", [P, 2, D], F32, c)
            h2T = sb("h2T", [P, 2, NK, P], F32, c)
            sq = sb("sqD", [P, D], F32, c)
            ss = sb("ss", [P, 2, 1], F32, c)
            rs = sb("rsD", [P, 2, 1], F32, c)
            wr = sb("wr", [P, NK, E], F32, c)
            ops = [ps(f"opsD{i}", [P, 1024], c) for i in range(2)]
            trs = ps("trs", [P, 1024], c)
            lg = ps("lg", [P, 512], c)
            d_raw = [sem(f"d_raw{i}") for i in range(NW)]
            d_wr, d_cat, d_x = sem("d_wr"), [sem("d_cat0"), sem("d_cat1")], [sem("d_res0"), sem("d_res1")]
            d_hi, d_lo, d_ones, d_diag, d_bc, d_bcc = (sem("d_hi"), sem("d_lo"), sem("d_ones"), sem("d_diag"),
                                                       sem("d_bc"), sem("d_bcc"))
            d_chi, d_clo = sem("d_chi"), sem("d_clo")
            d_mm, d_gx, d_x1 = sem("d_mm"), sem("d_gx"), sem("d_x1")
            d_sq, d_ms, d_rs, d_xn = sem("d_sq"), sem("d_ms"), sem("d_rs"), sem("d_xn")
            d_st = [sem("d_st0"), sem("d_st1")]
            d_tr, d_h2, d_lg, d_lc = sem("d_tr"), sem("d_h2"), sem("d_lg"), sem("d_lc")
            catv = catT.rearrange("(k p) n -> p k n", p=P)

            def schedule(eng, step):
                step(0, 0)
                step(1, 1)
                with eng.Fori(1, 4) as i:
                    step(2 * i, 0)
                    step(2 * i + 1, 1)
                for n in range(8, T + 2):
                    step(n, n % 2)

            def inside(n, m):
                return 0 <= n + m < T if isinstance(n, int) else True

            def group(n, m):
                return req(n + m) if isinstance(n, int) else 0

            with nc.Block() as block:
                @block.sync
                def _(sp):
                    for sm in d_st:
                        sp.sem_inc(sm, 32)
                    sp.dma_start(wr[:], io["w_router"][0].rearrange("(k p) e -> p k e", p=P)).then_inc(d_wr, 16)
                    for n in range(2):
                        sp.dma_start(rawc[:, n, :, :], catv[:, :, n * P:(n + 1) * P]).then_inc(d_cat[n], 16)
                    for k in range(NK):
                        if k >= NW:
                            sp.wait_ge(d_lo, k - NW + 1)
                        sp.dma_start(rawo[:, k % NW, :], io["w_out"][0, k * P:(k + 1) * P, :]).then_inc(d_raw[k % NW], 16)

                    def step(n, slot):
                        if inside(n, 0):
                            if not isinstance(n, int) or n >= 2:
                                sp.wait_ge(d_x1, n - 1)
                            if isinstance(n, int) and n >= TS:
                                src = io["x_prompt"][0, (n - TS) * P:(n - TS + 1) * P, :]
                            else:
                                src = io["x_sample"][0, bass.ds(n * P, P), :]
                            sp.dma_start(xt[:, slot, :], src).then_inc(d_x[slot], 16)
                        if inside(n, 2) and (not isinstance(n, int)):
                            sp.wait_ge(d_clo, 2 + n + 1)
                            sp.dma_start(rawc[:, slot, :, :], catv[:, :, bass.ds((n + 2) * P, P)]).then_inc(d_cat[slot], 16)
                        elif inside(n, 2):
                            sp.wait_ge(d_clo, 2 + n + 1)
                            sp.dma_start(rawc[:, slot, :, :], catv[:, :, (n + 2) * P:(n + 3) * P]).then_inc(d_cat[slot], 16)
                        if inside(n, -1):
                            sp.wait_ge(d_xn, n)
                            for dst, src in ((acc, x1), (xn2, xn)):
                                sp.dma_start(dst[bass.ds((n - 1) * P, P), :], src[:, 1 - slot, :]).then_inc(d_st[1 - slot], 16)

                    schedule(sp, step)
                    for sm in d_st:
                        sp.wait_ge(sm, 32 + 32 * T // 2)

                @block.tensor
                def _(pe):
                    pe.sem_inc(d_mm, 2)
                    pe.sem_inc(d_tr, 2)
                    pe.sem_inc(d_lg, 2)
                    pe.wait_ge(d_ones, 1)
                    for n in range(4 * NK):
                        if n >= 2 * NK:
                            pe.wait_ge(d_bcc, n // NK - 1)
                        pe.wait_ge(d_diag, n + 1)
                        pe.matmul(ops[n // NK % 2][:, n % NK * P:(n % NK + 1) * P], ones[:], diag[:, n % 2, :],
                                  start=True, stop=True).then_inc(d_bc, 1)
                    pe.wait_ge(d_bcc, 4)
                    pe.wait_ge(d_lo, NK)
                    pe.wait_ge(d_wr, 16)

                    def step(n, slot):
                        if inside(n, 0):
                            pe.wait_ge(d_clo, 2 + n + 1)
                            pe.wait_ge(d_gx, n + 1)
                            for half in range(2):
                                for k in range(NK):
                                    for a, b in ((0, 0), (0, 1), (1, 0)):
                                        mm = pe.matmul(ops[slot][:, half * 512:(half + 1) * 512], ca[a][:, slot, k, :],
                                                       wo[b][:, k, half * 512:(half + 1) * 512],
                                                       start=(k == 0 and a == b), stop=(k == NK - 1 and a == 1))
                            mm.then_inc(d_mm, 1)
                        if inside(n, -2):
                            t = n - 2
                            pe.wait_ge(d_xn, t + 1)
                            pe.wait_ge(d_h2, t + 1)
                            for k in range(NK):
                                mm = pe.transpose(trs[:, k * P:(k + 1) * P], xn[:, slot, k * P:(k + 1) * P], ident[:])
                            mm.then_inc(d_tr, 1)
                            pe.wait_ge(d_h2, 1 + t + 1)
                            pe.wait_ge(d_lc, t + 1)
                            for k in range(NK):
                                mm = pe.matmul(lg[:, 0:E], h2T[:, slot, k, :], wr[:, k, :], start=(k == 0), stop=(k == NK - 1))
                            mm.then_inc(d_lg, 1)

                    schedule(pe, step)

                @block.scalar
                def _(act):
                    for sm, n in ((d_chi, 2), (d_h2, 1), (d_lc, 1)):
                        act.sem_inc(sm, n)
                    for k in range(NK):
                        act.wait_ge(d_raw[k % NW], 16 * (k // NW + 1))
                        act.activation(wo[0][:, k, :], rawo[:, k % NW, :], ACT.Copy).then_inc(d_hi, 1)
                        if k % 2:
                            act.wait_ge(d_bc, NK * (k // 2 + 1))
                            act.activation(gates[k // 4][:, k // 2 % 2, :], ops[k // 2 % 2][:], ACT.Copy).then_inc(d_bcc, 1)

                    def split(m, slot):
                        act.wait_ge(d_cat[slot], 8 * (m - slot) + 16)
                        act.wait_ge(d_mm, m + 1)
                        act.activation(ca[0][:, slot, :, :], rawc[:, slot, :, :], ACT.Copy).then_inc(d_chi, 1)

                    split(0, 0)

                    def step(n, slot):
                        if inside(n, 1):
                            split(n + 1, 1 - slot)
                        if inside(n, -1):
                            act.wait_ge(d_x1, n)
                            act.activation(sq[:], x1[:, 1 - slot, :], ACT.Square,
                                           accum_out=ss[:, 1 - slot, :]).then_inc(d_sq, 1)
                        if inside(n, -2):
                            t, r = n - 2, group(n, -2)
                            act.wait_ge(d_tr, 2 + t + 1)
                            act.wait_ge(d_lg, t + 1)
                            for k in range(NK):
                                op = act.activation(h2T[:, slot, k, :], trs[:, k * P:(k + 1) * P], ACT.Identity,
                                                    bias=modT[:, 3, k, r:r + 1], scale=scaleA[:, 1, k, r:r + 1])
                            op.then_inc(d_h2, 1)
                            waits(act, (d_lg, 2 + t + 1))
                            act.activation(L[:, bass.ds(t, 1), :], lg[:, 0:E].unsqueeze(1), ACT.Copy).then_inc(d_lc, 1)

                    schedule(act, step)

                @block.vector
                def _(dve):
                    dve.sem_inc(d_clo, 2)
                    dve.sem_inc(d_gx, 2)
                    dve.memset(ones[:], 1.0).then_inc(d_ones, 1)
                    for k in range(NK):
                        for n in range(4 * k, 4 * k + 4):
                            if n >= 2:
                                dve.wait_ge(d_bc, n - 1)
                            which, r = (2, 5)[n // (2 * NK)], n // NK % 2
                            dve.tensor_scalar(diag[:, n % 2, :], ident[:], modT[:, which, n % NK, r:r + 1], None,
                                              ALU.mult).then_inc(d_diag, 1)
                        dve.wait_ge(d_hi, k + 1)
                        dve.tensor_tensor(wo[1][:, k, :], rawo[:, k % NW, :], wo[0][:, k, :].bitcast(F32),
                                          ALU.subtract).then_inc(d_lo, 1)
                    dve.wait_ge(d_bcc, 4)

                    def split(m, slot):
                        dve.wait_ge(d_chi, 2 + m + 1)
                        dve.tensor_tensor(ca[1][:, slot, :, :], rawc[:, slot, :, :], ca[0][:, slot, :, :].bitcast(F32),
                                          ALU.subtract).then_inc(d_clo, 1)

                    split(0, 0)

                    def step(n, slot):
                        if inside(n, 1):
                            split(n + 1, 1 - slot)
                        if inside(n, -1):
                            t, r, at = n - 1, group(n, -1), 1 - slot
                            dve.wait_ge(d_mm, 2 + t + 1)
                            dve.wait_ge(d_st[at], 16 * (t - at) + 32)
                            dve.tensor_tensor(x1[:, at, :], ops[at][:], gates[0][:, r, :],
                                              ALU.mult).then_inc(d_gx, 1)
                            dve.wait_ge(d_rs, t + 1)
                            dve.tensor_scalar(xn[:, at, :], x1[:, at, :], rs[:, at, :], None, ALU.mult).then_inc(d_xn, 1)

                    schedule(dve, step)

                @block.gpsimd
                def _(gp):
                    def step(n, slot):
                        if inside(n, -1):
                            t, at = n - 1, 1 - slot
                            gp.wait_ge(d_x[at], 8 * (t - at) + 16)
                            gp.wait_ge(d_gx, 2 + t + 1)
                            gp.tensor_tensor(x1[:, at, :], x1[:, at, :], xt[:, at, :], ALU.add).then_inc(d_x1, 1)
                            waits(gp, (d_sq, t + 1))
                            gp.tensor_scalar(ss[:, at, :], ss[:, at, :], 1.0 / D, EPS, ALU.mult, ALU.add).then_inc(d_ms, 1)
                            gp.wait_ge(d_ms, t + 1)
                            gp.tensor_tensor(rs[:, at, :], ss[:, at, :], nhalf[:, 0:1], ALU.pow).then_inc(d_rs, 1)

                    schedule(gp, step)

        idxT = sb("idxT", [P, 48], I32)
        gT = sb("gT", [P, 48])
        with ExitStack() as c:
            mx = sb("mx", [P, T], F32, c)
            sm_ = sb("sm", [P, T], F32, c)
            affP = sb("affP", [P, TS, 48], F32, c)
            top = sb("top", [48, N_S], F32, c)
            vals = sb("topv", [48, P], F32, c)
            idxu = sb("topi", [48, P], U32, c)
            idxf = sb("idxf", [48, P], F32, c)
            tb = ps("tb", [48, 1024], c)
            ti, tv = ps("ti", [P, 512], c), ps("tv", [P, 512], c)
            e_v, e_exp, e_aff, e_tb, e_t, e_f, e_tt, e_dbg = (sem("e_v"), sem("e_exp"), sem("e_aff"), sem("e_tb"),
                                                            sem("e_t"), sem("e_f"), sem("e_tt"), sem("e_dbg"))
            ROUNDS = CS // 8
            with nc.Block() as block:
                @block.scalar
                def _(act):
                    act.wait_ge(e_v, 2)
                    act.activation(L[:], L[:], ACT.Exp).then_inc(e_exp, 1)

                @block.tensor
                def _(pe):
                    pe.wait_ge(e_aff, 1)
                    for t in range(TS):
                        mm = pe.transpose(tb[:, t * P:(t + 1) * P], affP[:, t, :], ident[:])
                    mm.then_inc(e_tb, 1)
                    pe.wait_ge(e_f, 2)
                    pe.transpose(ti[:, 0:48], idxf[:], ident[0:48, 0:48])
                    pe.transpose(tv[:, 0:48], vals[:], ident[0:48, 0:48]).then_inc(e_tt, 1)

                @block.vector
                def _(dve):
                    count = [0]

                    def own(op):
                        count[0] += 1
                        op.then_inc(e_v, 1)
                        dve.wait_ge(e_v, count[0])

                    own(dve.tensor_reduce(mx[:], L[:], AX.X, ALU.max))
                    own(dve.tensor_tensor(L[:], L[:], mx[:].unsqueeze(2).broadcast_to([P, T, E]), ALU.subtract))
                    own(dve.memset(affP[:], -1.0))
                    dve.wait_ge(e_exp, 1)
                    own(dve.tensor_reduce(sm_[:], L[:], AX.X, ALU.add))
                    own(dve.reciprocal(sm_[:], sm_[:]))
                    rcp = sm_[:].unsqueeze(2).broadcast_to([P, T, E])
                    dve.tensor_tensor(affP[:, :, 0:E], L[:, 0:TS, :], rcp[:, 0:TS, :], ALU.mult)
                    dve.tensor_tensor(affP[:, 0:TP, 32:48], L[:, TS:T, :], rcp[:, TS:T, :], ALU.mult).then_inc(e_aff, 1)
                    dve.wait_ge(e_tb, 1)
                    own(dve.tensor_copy(top[:], tb[:]))
                    for n in range(ROUNDS):
                        v = vals[:, 8 * n:8 * n + 8]
                        own(dve.max(v, top[:]))
                        own(dve.max_index(idxu[:, 8 * n:8 * n + 8], v, top[:]))
                        if n < ROUNDS - 1:
                            own(dve.match_replace(top[:], v, top[:], -1.0))
                    own(dve.tensor_copy(idxf[:], idxu[:]))
                    dve.tensor_copy(vals[32:48, CP:2 * CP], vals[32:48, 0:CP]).then_inc(e_f, 1)
                    dve.tensor_scalar(idxf[32:48, :], idxf[32:48, :], float(N_S), None, ALU.add).then_inc(e_f, 1)
                    dve.wait_ge(e_tt, 1)
                    dve.tensor_copy(idxT[:], ti[:, 0:48])
                    dve.tensor_copy(gT[:], tv[:, 0:48]).then_inc(e_t, 1)

                if "vals" in io:
                    @block.sync
                    def _(sp):
                        sp.wait_ge(e_t, 1)
                        sp.dma_start(io["vals"], vals[:]).then_inc(e_dbg, 16)
                        sp.dma_start(io["idx"], idxf[:]).then_inc(e_dbg, 16)
                        sp.dma_start(io["dbg"], L[:]).then_inc(e_dbg, 16)
                        sp.wait_ge(e_dbg, 48)
        if stop_after in "DE":
            return

        with ExitStack() as c:
            RING = 3
            G_, U_, D_ = 0, 1, 2
            raw = sb("rawW", [P, RING, 3, NK * W_STEP], F32, c)
            wGU = [[sb(f"w{n}_{x}", [P, NK, W_STEP], F32R, c) for x in ("hi", "lo")] for n in "GU"]
            wD = [sb(f"wD_{x}", [P, 2, 2, D], F32R, c) for x in ("hi", "lo")]
            X = sb("X", [P, NK, 2 * C], F32R, c)
            xm = sb("xm", [P, NK, C], F32, c)
            hid = sb("hid", [P, 2, 2, 2 * C], F32R, c)
            gl, ga, sg = sb("gl", [P, 2, C], F32, c), sb("ga", [P, 2, C], F32, c), sb("sg", [P, 2, C], F32, c)
            ul, ua, hf = sb("ul", [P, 2, C], F32, c), sb("ua", [P, 2, C], F32, c), sb("hf", [P, 2, C], F32, c)
            yp = sb("yp", [CP, D], F32, c)
            xg = [sb("xgS", [CS, D], F32, c), sb("xgP", [CP, D], F32, c)]
            ys = [sb("ysS", [CS, D], F32, c), sb("ysP", [CP, D], F32, c)]
            gi, si = sb("gi", [P, 2], I32, c), sb("si", [P, 2], I32, c)
            gc = sb("gc", [P, 2], F32, c)
            psG, psU = ps("psG", [P, 2, 512], c), ps("psU", [P, 2, 512], c)
            psS = ps("psS", [CS, 2, 512], c)
            psP = ps("psP", [2 * CP, 2, 512], c)
            XT = slice(2 * C, 3 * C)
            f_raw = [[sem(f"f_raw{n}{j}") for j in range(RING)] for n in "GUD"]
            f_hi, f_lo = [sem(f"f_hi{n}") for n in "GUD"], [sem(f"f_lo{n}") for n in "GUD"]
            f_g, f_u, f_d = sem("f_g"), sem("f_u"), sem("f_d")
            f_gl, f_ga, f_sg = sem("f_gl"), sem("f_ga"), sem("f_sg")
            f_ul, f_ua, f_hf = sem("f_ul"), sem("f_ua"), sem("f_hf")
            f_hh, f_hl = sem("f_hh"), sem("f_hl")
            f_gi, f_si, f_got, f_xt, f_xm = sem("f_gi"), sem("f_si"), sem("f_got"), sem("f_xt"), sem("f_xm")
            f_xh, f_x, f_y, f_ys, f_sc = sem("f_xh"), sem("f_x"), sem("f_y"), sem("f_ys"), sem("f_sc")
            f_sum, f_free = sem("f_sum"), sem("f_free")
            USES = [len(range(j, STEPS, RING)) for j in range(RING)]
            LAST = [max(range(j, STEPS, RING)) for j in range(RING)]
            wg_ = io["w_gate"][0].rearrange("e (k p) f -> p e k f", p=P)
            wu_ = io["w_up"][0].rearrange("e (k p) f -> p e k f", p=P)
            wd_ = io["w_down"][0].rearrange("e (s f p) d -> p e s f d", p=P, f=2)
            pair = lambda t, e: t[:].rearrange("p (a e) -> p a e", e=E)[:, 0:3:2, bass.ds(e, 1)]

            def experts(eng, body):
                body(0, True, False)
                with eng.Fori(1, E - 1) as e:
                    body(e, False, False)
                body(E - 1, False, True)

            def raw_ready(eng, kind, e, i):
                eng.wait_ge(f_raw[kind][i % RING], 16 * (USES[i % RING] * e + i // RING + 1))

            def split_part(kind, i, half, part):
                a, b = half * NK * W_STEP // 2, (half + 1) * NK * W_STEP // 2
                if kind == D_:
                    dst = wD[part][:, i % 2, half, :]
                else:
                    dst = wGU[kind][part][:, half * NK // 2:(half + 1) * NK // 2, :].rearrange("p k f -> p (k f)")
                return dst, raw[:, i % RING, kind, a:b]

            def lo_half(eng, kind, e, i, half):
                eng.wait_ge(f_hi[kind], 2 * (STEPS * e + i) + half + 1)
                (hi, src), (lo, _) = split_part(kind, i, half, 0), split_part(kind, i, half, 1)
                eng.tensor_tensor(lo, src, hi.bitcast(F32), ALU.subtract).then_inc(f_lo[kind], 1)

            def following(e, i):
                return (e, i + 1) if i + 1 < STEPS else (e + 1, 0)

            with nc.Block() as block:
                @block.sync
                def _(sp):
                    def body(e, first, last):
                        for i in range(STEPS):
                            s = STEPS * e + i
                            for kind in (G_, U_, D_):
                                if not first or i >= RING:
                                    back = RING if i >= RING else STEPS + i - LAST[i]
                                    sp.wait_ge(f_lo[kind], 2 * (s - back + 1))
                                dst = raw[:, i % RING, kind, :]
                                if kind == D_:
                                    sp.dma_start(dst.rearrange("p (f d) -> p f d", f=2),
                                                 wd_[:, bass.ds(e, 1), i, :, :].rearrange("p e f d -> p (e f) d")
                                                 ).then_inc(f_raw[kind][i % RING], 16)
                                else:
                                    src = (wg_, wu_)[kind][:, bass.ds(e, 1), :, i * W_STEP:(i + 1) * W_STEP]
                                    sp.dma_start(dst.rearrange("p (k f) -> p k f", k=NK),
                                                 src.rearrange("p e k f -> p (e k) f")).then_inc(f_raw[kind][i % RING], 16)

                    experts(sp, body)

                @block.tensor
                def _(pe):
                    pe.sem_inc(f_d, 2)

                    def gate_or_up(kind, out, e, i):
                        s = STEPS * e + i
                        for k in range(NK):
                            if k in (0, NK // 2):
                                pe.wait_ge(f_lo[kind], 2 * s + (1 if k == 0 else 2))
                            for f in range(2):
                                hi, lo = (wGU[kind][x][:, k, f * P:(f + 1) * P] for x in range(2))
                                pe.matmul(out[:, f, 0:2 * C], hi, X[:, k, :], start=(k == 0), stop=False,
                                          skip_group_check=True)
                                mm = pe.matmul(out[:, f, 0:C], lo, X[:, k, 0:C], start=False, stop=(k == NK - 1),
                                               skip_group_check=True)
                        return mm

                    def down(e, i):
                        s = STEPS * e + i
                        pe.wait_ge(f_hl, 1 + s + 1)
                        if i == 0:
                            pe.wait_ge(f_y, e + 1)
                        for f in range(2):
                            pe.wait_ge(f_lo[D_], 2 * s + f + 1)
                            h = hid[:, i % 2, f, :]
                            latent_hi, latent_lo, context_hi, context = (h[:, 0:CS], h[:, C + CP:2 * C],
                                                                         h[:, CS:C], h[:, CS:C + CP])
                            for w, out, x in ((0, psS, latent_hi), (0, psS, latent_lo), (0, psP, context),
                                              (1, psS, latent_hi), (1, psP[0:CP], context_hi)):
                                for half in range(2):
                                    mm = pe.matmul(out[:, half, :], x, wD[w][:, i % 2, f, half * 512:(half + 1) * 512],
                                                   start=(i == 0 and f == 0 and w == 0 and x is not latent_lo),
                                                   stop=(i == STEPS - 1 and f == 1 and w == 1), skip_group_check=True)
                        mm.then_inc(f_d, 1)

                    def transpose_rows(k, bank):
                        out = psU[:, bank, XT]
                        pe.transpose(out[:, 0:CS], xg[0][:, k * P:(k + 1) * P], ident[:])
                        return pe.transpose(out[:, CS:C], xg[1][:, k * P:(k + 1) * P], ident[0:CP, 0:CP])

                    pe.wait_ge(f_got, 32)
                    for k in range(NK):
                        if k >= 2:
                            pe.wait_ge(f_xm, k - 1)
                        transpose_rows(k, k % 2).then_inc(f_xt, 1)

                    def body(e, first, last):
                        for i in range(STEPS):
                            s = STEPS * e + i
                            if i == 0:
                                pe.wait_ge(f_x, 2 * e + 2)
                            pe.wait_ge(f_ga, s + 1)
                            gate_or_up(G_, psG, e, i).then_inc(f_g, 1)
                            pe.wait_ge(f_ua, s + 1)
                            if i > STEPS - NK and not last:
                                pe.wait_ge(f_xm, NK * (e + 1) + i - (STEPS - NK))
                            if i == 0:
                                pe.wait_ge(f_xm, NK * (e + 1))
                            mm = gate_or_up(U_, psU, e, i)
                            if i >= STEPS - NK and not last:
                                if i == STEPS - NK:
                                    pe.wait_ge(f_got, 32 * (e + 2))
                                mm = transpose_rows(i - (STEPS - NK), 0)
                            mm.then_inc(f_u, 1)
                            if i:
                                down(e, i - 1)
                        down(e, STEPS - 1)

                    experts(pe, body)

                @block.scalar
                def _(act):
                    act.sem_inc(f_y, 1)

                    def hi(kind, e, i, halves=(0, 1)):
                        raw_ready(act, kind, e, i)
                        for half in halves:
                            dst, src = split_part(kind, i, half, 0)
                            act.activation(dst, src, ACT.Copy).then_inc(f_hi[kind], 1)

                    def x_hi(e):
                        act.wait_ge(f_xm, NK * (e + 1))
                        for half in range(2):
                            a, b = half * NK // 2, (half + 1) * NK // 2
                            act.activation(X[:, a:b, 0:C], xm[:, a:b, :], ACT.Copy).then_inc(f_xh, 1)

                    def take_y(e):
                        act.wait_ge(f_d, 2 + STEPS * e)
                        act.wait_ge(f_si, e)
                        for dst, src, scale in ((ys[0], psS[:], gc[:, 0:1]), (ys[1], psP[0:CP], 1.0),
                                                (yp, psP[CP:2 * CP], 1.0)):
                            op = act.activation(dst[:].rearrange("p (a d) -> p a d", a=2), src, ACT.Copy, scale=scale)
                        op.then_inc(f_y, 1)

                    hi(G_, 0, 0)
                    hi(U_, 0, 0)
                    x_hi(0)

                    def body(e, first, last):
                        for i in range(STEPS):
                            s, n = STEPS * e + i, following(e, i)
                            end = last and i == STEPS - 1
                            act.wait_ge(f_g, s + 1)
                            act.activation(gl[:], psG[:, :, C:2 * C], ACT.Copy).then_inc(f_gl, 1)
                            if not end:
                                hi(G_, *n)
                            act.wait_ge(f_ga, 1 + s + 1)
                            act.activation(sg[:], ga[:], ACT.Silu).then_inc(f_sg, 1)
                            act.wait_ge(f_u, s + 1)
                            act.activation(ul[:], psU[:, :, C:2 * C], ACT.Copy).then_inc(f_ul, 1)
                            if not end:
                                hi(U_, *n, halves=(0,) if i == STEPS - 1 else (0, 1))
                            act.wait_ge(f_hf, s + 1)
                            act.activation(hid[:, i % 2, :, 0:C], hf[:], ACT.Copy).then_inc(f_hh, 1)
                            if i == STEPS - 1 and not last:
                                x_hi(e + 1)
                                hi(U_, *n, halves=(1,))
                            if i == 0 and not first:
                                take_y(e)

                    experts(act, body)
                    take_y(E)

                @block.vector
                def _(dve):
                    for sm in (f_ga, f_ua, f_hl):
                        dve.sem_inc(sm, 1)
                    dve.tensor_copy(gi[:].unsqueeze(2), pair(idxT, 0)).then_inc(f_gi, 1)

                    def x_mod(k, bank):
                        src = psU[:, bank, XT]
                        for r, a, b in ((0, 0, CS), (1, CS, C)):
                            op = dve.tensor_scalar(xm[:, k, a:b], src[:, a:b], scaleA[:, 1, k, r:r + 1],
                                                   modT[:, 3, k, r:r + 1], ALU.mult, ALU.add)
                        return op

                    def x_lo(e):
                        for half in range(2):
                            dve.wait_ge(f_xh, 2 * e + half + 1)
                            a, b = half * NK // 2, (half + 1) * NK // 2
                            dve.tensor_tensor(X[:, a:b, C:2 * C], xm[:, a:b, :], X[:, a:b, 0:C].bitcast(F32),
                                              ALU.subtract).then_inc(f_x, 1)

                    def for_scatter(e):
                        dve.wait_ge(f_free, e)
                        dve.tensor_copy(si[:].unsqueeze(2), pair(idxT, e - 1))
                        dve.tensor_copy(gc[:].unsqueeze(2), pair(gT, e - 1)).then_inc(f_si, 1)

                    def down_hi(e, i, s):
                        dve.wait_ge(f_d, s + (1 if i else 2))
                        raw_ready(dve, D_, e, i)
                        for half in range(2):
                            dst, src = split_part(D_, i, half, 0)
                            dve.tensor_copy(dst, src).then_inc(f_hi[D_], 1)

                    for k in range(NK):
                        dve.wait_ge(f_xt, k + 1)
                        x_mod(k, k % 2).then_inc(f_xm, 1)
                    for kind in (G_, U_):
                        for half in range(2):
                            lo_half(dve, kind, 0, 0, half)
                    x_lo(0)

                    def body(e, first, last):
                        for i in range(STEPS):
                            s, n = STEPS * e + i, following(e, i)
                            end = last and i == STEPS - 1
                            if i == 0 and not last:
                                dve.tensor_copy(gi[:].unsqueeze(2), pair(idxT, e + 1)).then_inc(f_gi, 1)
                            dve.wait_ge(f_gl, s + 1)
                            dve.tensor_tensor(ga[:], psG[:, :, 0:C], gl[:], ALU.add).then_inc(f_ga, 1)
                            if i == 0 and not first:
                                for_scatter(e)
                            final = i == STEPS - 1
                            if final:
                                down_hi(e, i, s)
                            for half in range(1 if final else 2):
                                if not end:
                                    lo_half(dve, G_, *n, half)
                            if not final:
                                down_hi(e, i, s)
                            dve.wait_ge(f_ul, s + 1)
                            dve.tensor_tensor(ua[:], psU[:, :, 0:C], ul[:], ALU.add).then_inc(f_ua, 1)
                            dve.wait_ge(f_ua, 1 + s + 1)
                            dve.wait_ge(f_sg, s + 1)
                            dve.wait_ge(f_hl, s + 1)
                            dve.tensor_tensor(hf[:], sg[:], ua[:], ALU.mult).then_inc(f_hf, 1)
                            if not end:
                                if final:
                                    lo_half(dve, G_, *n, 1)
                                else:
                                    for half in range(2 if i == 0 else 1):
                                        lo_half(dve, U_, *n, half)
                            dve.wait_ge(f_hh, s + 1)
                            for dst, a, b in ((C, CS, C), (C + CP, 0, CS)):
                                op = dve.tensor_tensor(hid[:, i % 2, :, dst:dst + b - a], hf[:, :, a:b],
                                                       hid[:, i % 2, :, a:b].bitcast(F32), ALU.subtract)
                            op.then_inc(f_hl, 1)
                            if i >= STEPS - NK and not last:
                                x_mod(i - (STEPS - NK), 0).then_inc(f_xm, 1)
                            if final and not last:
                                x_lo(e + 1)
                            if not end and i:
                                for half in range(0 if final else 1, 2):
                                    lo_half(dve, U_, *n, half)

                    experts(dve, body)
                    for_scatter(E)

                @block.gpsimd
                def _(gp):
                    gp.sem_inc(f_free, 1)

                    def gather(e):
                        waits(gp, (f_gi, e + 1))
                        for r, n in ((0, CS), (1, CP)):
                            gp.indirect_dma_start(xg[r][:], None, xn2[:], bass.IndirectOffsetOnAxis(ap=gi[0:n, r:r + 1], axis=0)
                                                  ).then_inc(f_got, 16)

                    def finish_context(e):
                        gp.wait_ge(f_y, 1 + e)
                        gp.tensor_tensor(ys[1][:], ys[1][:], yp[:], ALU.add).then_inc(f_sum, 1)
                        waits(gp, (f_sum, 2 * e - 1))
                        gp.tensor_scalar(ys[1][:], ys[1][:], gc[0:CP, 1:2], None, ALU.mult).then_inc(f_sum, 1)

                    def scatter(e):
                        gp.wait_ge(f_sum, 2 * e)
                        gp.tensor_tensor(ys[1][:], ys[1][:], gates[1][0:CP, 1, :], ALU.mult)
                        gp.tensor_tensor(ys[0][:], ys[0][:], gates[1][:, 0, :], ALU.mult).then_inc(f_ys, 1)
                        waits(gp, (f_ys, e))
                        for r, n in ((0, CS), (1, CP)):
                            gp.indirect_dma_start(acc[:], bass.IndirectOffsetOnAxis(ap=si[0:n, r:r + 1], axis=0), ys[r][:], None,
                                                  compute_op=ALU.add).then_inc(f_sc, 16)

                    gather(0)

                    def body(e, first, last):
                        for i in range(STEPS):
                            if i == 0 and not last:
                                gp.wait_ge(f_xt, NK)
                                if not first:
                                    gp.wait_ge(f_u, STEPS * e)
                                gather(e + 1)
                            for half in range(2):
                                lo_half(gp, D_, e, i, half)
                            if i == 0 and not first:
                                finish_context(e)
                            if i == 1 and not first:
                                scatter(e)
                            if i == 3 and not first:
                                gp.wait_ge(f_sc, 32 * e)
                                gp.sem_inc(f_free, 1)

                    experts(gp, body)
                    finish_context(E)
                    scatter(E)
                    gp.wait_ge(f_sc, 32 * E)

        with ExitStack() as c:
            xf = sb("xf", [P, T, D], F32, c)
            gf = sb("gf", [P, D], F32, c)
            sq = sb("sqG", [P, 2, D], F32, c)
            ss, rs = sb("ssG", [P, T], F32, c), sb("rsG", [P, T], F32, c)
            g_g, g_x = sem("g_g"), a_x
            g_sq, g_ms, g_rs, g_y, g_out = sem("g_sq"), sem("g_ms"), sem("g_rs"), sem("g_y"), sem("g_out")
            with nc.Block() as block:
                @block.sync
                def _(sp):
                    for t in range(T):
                        sp.dma_start(xf[:, t, :], acc[t * P:(t + 1) * P, :]).then_inc(g_x[t], 16)
                        if t == 0:
                            sp.dma_start(gf[:], io["final_g"].rearrange("(a d) -> a d", a=1).broadcast_to([P, D])
                                         ).then_inc(g_g, 16)
                    for t in range(T):
                        sp.wait_ge(g_y, t + 1)
                        dst = (io["y_sample"][0, t * P:(t + 1) * P, :] if t < TS else
                               io["y_prompt"][0, (t - TS) * P:(t - TS + 1) * P, :])
                        sp.dma_start(dst, xf[:, t, :]).then_inc(g_out, 16)
                    sp.wait_ge(g_out, 16 * T)

                @block.scalar
                def _(act):
                    for t in range(T):
                        act.wait_ge(g_x[t], 32)
                        if t >= 2:
                            act.wait_ge(g_sq, t - 1)
                        act.activation(sq[:, t % 2, :], xf[:, t, :], ACT.Square, accum_out=ss[:, t:t + 1]).then_inc(g_sq, 1)

                @block.gpsimd
                def _(gp):
                    for t in range(T):
                        gp.wait_ge(g_sq, t + 1)
                        gp.tensor_scalar(ss[:, t:t + 1], ss[:, t:t + 1], 1.0 / D, EPS, ALU.mult, ALU.add).then_inc(g_ms, 1)
                        gp.wait_ge(g_ms, t + 1)
                        gp.tensor_tensor(rs[:, t:t + 1], ss[:, t:t + 1], nhalf[:, 0:1], ALU.pow).then_inc(g_rs, 1)

                @block.vector
                def _(dve):
                    dve.wait_ge(g_g, 16)
                    for t in range(T):
                        dve.wait_ge(g_rs, t + 1)
                        dve.scalar_tensor_tensor(xf[:, t, :], xf[:, t, :], rs[:, t:t + 1], gf[:], ALU.mult,
                                                 ALU.mult).then_inc(g_y, 1)


_OUT = [("y_prompt", (1, N_P, D)), ("y_sample", (1, N_S, D)), ("state_out", (1, 1, 2, H, P, P))]


def kernel(x_prompt, x_sample, state_ret, c, c_ctx, norm1_g, norm2_g, final_g, w_mod, b_mod,
           w_in, w_fmix, w_out, w_router, w_gate, w_up, w_down):
    import concourse.bacc as bacc
    from concourse.bass_utils import run_bass_kernel_spmd

    ins = dict(x_prompt=x_prompt, x_sample=x_sample, state_ret=state_ret, c=c, c_ctx=c_ctx, norm1_g=norm1_g,
               norm2_g=norm2_g, final_g=final_g, w_mod=w_mod, b_mod=b_mod, w_in=w_in, w_fmix=w_fmix, w_out=w_out,
               w_router=w_router, w_gate=w_gate, w_up=w_up, w_down=w_down)
    arrays = {f"in_{k}": np.asarray(v) for k, v in {**ins, **tables()}.items()}
    nc = bacc.Bacc("TRN2", target_bir_lowering=False, num_devices=1)
    io = {k[3:]: nc.dram_tensor(k, v.shape, mybir.dt.from_np(v.dtype), kind="ExternalInput").ap() for k, v in arrays.items()}
    for k, shape in _OUT:
        io[k] = nc.dram_tensor(k, shape, F32, kind="ExternalOutput").ap()
    build(nc, io)
    nc.finalize()
    res = run_bass_kernel_spmd(nc, [arrays], core_ids=[0]).results[0]
    return res["y_prompt"], res["y_sample"], res["state_out"]
```

```python
import numpy as np
import concourse.bass as bass
from concourse import mybir
from contextlib import ExitStack

F32 = mybir.dt.float32
F32R = mybir.dt.float32r
I32 = mybir.dt.int32
U32 = mybir.dt.uint32
ALU = mybir.AluOpType
ACT = mybir.ActivationFunctionType
AX = mybir.AxisListType

P = 128
D = 1024
NK = D // P
N_S, N_P = 1024, 256
N = N_S + N_P
TS, TP = N_S // P, N_P // P
T = TS + TP
H = 4
DIN = 3072
E = 16
FF = 2816
CS, CP = 2 * N_S // E, 2 * N_P // E
C = CS + CP
W_STEP = 256
STEPS = FF // W_STEP
EPS = 1e-6
SCALE = P ** -0.5


def tables():
    f8, f4 = np.float64, np.float32
    t = {}
    t["c_ident"] = np.eye(P)
    i = np.arange(P, dtype=f8)
    ang = 2 * np.pi * np.outer(i, i) / P
    t["c_chan"] = np.stack([np.cos(ang), -np.sin(ang)], 1) / np.sqrt(P)
    n, k = np.arange(N_S // 2 + 1, dtype=f8), np.arange(N_S // 2 + 1, dtype=f8)
    ang = 2 * np.pi * np.outer(n, k) / N_S
    t["c_poscos"] = np.cos(ang) / np.sqrt(N_S)
    t["c_possin"] = (np.sin(ang) / np.sqrt(N_S))[:N_S // 2, :N_S // 2]
    i2 = np.arange(N_P, dtype=f8)
    ang = 2 * np.pi * np.outer(i2, i2) / N_P
    t["c_ctxdft"] = np.stack([np.cos(ang), np.sin(ang)], 1) / np.sqrt(N_P)
    tok = np.arange(N_S)
    freqs = (f4(10000.0) ** (-np.arange(32, dtype=f4) / f4(32))).astype(f4)
    row = (tok // 64).astype(f4)[:, None] * freqs[None]
    col = (tok % 64).astype(f4)[:, None] * freqs[None]
    full = np.concatenate([row, row, col, col], 1).astype(f8)
    t["c_rope"] = np.stack([np.cos(full), np.sin(full)], 1)
    lg = np.stack([np.log(1.0 - 2.0 ** (-5.0 - np.arange(H))).astype(f4),
                   np.log(1.0 - 2.0 ** (-5.5 - np.arange(H))).astype(f4)], 1).astype(f8)
    j, q = i[:, None], i[None, :]
    mask = np.zeros((P, H, 2, P))
    qdec = np.zeros((P, H, 2, P))
    kdec = np.zeros((P, H, 2))
    for h in range(H):
        mask[:, h, 0] = np.where(q >= j, np.exp(lg[h, 0] * np.maximum(q - j, 0)), 0) * SCALE
        mask[:, h, 1] = np.where(j >= q, np.exp(lg[h, 1] * np.maximum(j - q, 0)), 0) * SCALE
        qdec[:, h, 0] = np.exp(lg[h, 0] * (i + 1))[None]
        qdec[:, h, 1] = np.exp(lg[h, 1] * (P - i))[None]
        kdec[:, h, 0] = np.exp(lg[h, 0] * (P - 1 - i)) * SCALE
        kdec[:, h, 1] = np.exp(lg[h, 1] * i) * SCALE
    t["c_mask"], t["c_qdec"], t["c_kdec"] = mask, qdec, kdec
    t["c_sdec"] = np.broadcast_to(np.exp(lg * P)[None], (P, H, 2))
    return {k: np.ascontiguousarray(v, f4) for k, v in t.items()}


def build(nc, io):
    ctx = ExitStack()
    with ctx:
        sems = []

        def sem(name):
            sems.append(nc.alloc_semaphore(name=name))
            return sems[-1]

        def sb(name, shape, dt=F32, c=ctx):
            return c.enter_context(nc.sbuf_tensor(name, shape, dt))

        def ps(name, shape, c, dt=F32):
            return c.enter_context(nc.psum_tensor(name, shape, dt))

        catT = nc.dram_tensor("catT", [D, N], F32).ap()
        acc = nc.dram_tensor("acc", [N, D], F32).ap()
        xn2 = nc.dram_tensor("xn2", [N, D], F32).ap()

        a_const = sem("a_const")
        ident = sb("ident", [P, P])
        vecT = sb("vecT", [P, 80])
        modT = sb("modT", [P, 6, NK, 2])
        scaleA = sb("scaleA", [P, 2, NK, 2])
        nhalf = sb("nhalf", [P, T])

        def x_rows(t):
            return io["x_sample"][0, t * P:(t + 1) * P, :] if t < TS else io["x_prompt"][0, (t - TS) * P:(t - TS + 1) * P, :]

        def waits(eng, *pairs):
            pairs = [(sm, v if isinstance(v, int) else eng.to_reg(v)) for sm, v in pairs]
            eng.wait_ge(a_const, 16)
            for sm, v in pairs:
                eng.wait_ge(sm, v)

        def req(t):
            return 0 if t < TS else 1

        stack_h, stack_w = ExitStack(), ExitStack()
        hT = [sb("hT_hi", [P, NK, N], F32R, stack_h), sb("hT_lo", [P, NK, N], F32R, stack_h)]
        NG = 4
        raw = sb("raw", [P, NG, 384], F32, stack_w)
        wq = [sb("wq_hi", [P, NK, 384], F32R, stack_w), sb("wq_lo", [P, NK, 384], F32R, stack_w)]
        b_raw = [sem(f"b_raw{i}") for i in range(NG)]
        b_hi, b_lo = sem("b_hi"), sem("b_lo")
        w_in_rows = io["w_in"][0].rearrange("(k p) (s c) -> k p s c", p=P, s=6)

        def row_tile(sp, h, k, gates, use):
            lo, hi = (4, 6) if gates else (1, 4)
            sp.wait_ge(b_hi, use + 1)
            sp.wait_ge(b_lo, use + 1)
            dst = raw[:, k % NG, 0:P * (hi - lo)].rearrange("p (s c) -> p s c", c=P)
            sp.dma_start(dst, w_in_rows[k, :, lo:hi, bass.ds(h * P, P)]).then_inc(b_raw[k % NG], 16)

        def qkv_hi(act, h, k):
            act.wait_ge(b_raw[k % NG], 16 * (4 * h + k // NG + 1))
            act.activation(wq[0][:, k, :], raw[:, k % NG, :], ACT.Copy).then_inc(b_hi, 1)

        def qkv_lo(dve, h, k):
            dve.wait_ge(b_hi, NG + 2 * NK * h + k + 1)
            dve.tensor_tensor(wq[1][:, k, :], raw[:, k % NG, :], wq[0][:, k, :].bitcast(F32),
                              ALU.subtract).then_inc(b_lo, 1)

        with ExitStack() as c:
            WR = 4
            COLS = 2 * D
            GM = 6 * D // COLS
            vecs = sb("vecs", [80, P], F32, c)
            x = sb("x", [P, T, D], F32, c)
            wm = sb("wm", [P, WR, COLS], F32, c)
            mrow = sb("mrow", [2, COLS], F32, c)
            cond = sb("cond", [P, NK, 2], F32, c)
            sq = sb("sq", [P, 2, D], F32, c)
            ssum = sb("ssum", [P, T], F32, c)
            rstd = sb("rstd", [P, T], F32, c)
            hfull = sb("hfull", [P, 2, 512], F32, c)
            mod = ps("mod", [2, 4, 512], c)
            small = ps("small", [P, 512], c)
            mps = small[:, 0:96].rearrange("p (j r) -> p j r", r=2)
            vps = small[:, 128:208]
            tps = [ps(f"tps{i}", [P, 512], c) for i in range(3)]
            a_x, a_vec = [sem(f"a_x{i}") for i in range(T)], sem("a_vec")
            a_w = [sem(f"a_w{i}") for i in range(WR)]
            a_vt, a_vtc, a_cond, a_wused, a_mod = sem("a_vt"), sem("a_vtc"), sem("a_cond"), sem("a_wused"), sem("a_mod")
            a_row, a_mt = sem("a_row"), sem("a_mt")
            a_sq, a_mean, a_rstd, a_xn = sem("a_sq"), sem("a_mean"), sem("a_rstd"), sem("a_xn")
            a_scale, a_tp, a_hi, a_full, a_lo = sem("a_scale"), sem("a_tp"), sem("a_hi"), sem("a_full"), sem("a_lo")
            a_half = sem("a_half")
            groups = [(k, g) for k in range(NK) for g in range(3)]

            def group_tiles(g):
                return range(4 * g, min(4 * g + 4, T))

            with nc.Block() as block:
                @block.sync
                def _(sp):
                    sp.dma_start(ident[:], io["c_ident"]).then_inc(a_const, 16)
                    rows = [(io["b_mod"][0].rearrange("(j p) -> j p", p=P), 0, 48),
                            (io["norm1_g"][0].rearrange("(j p) -> j p", p=P), 48, 8),
                            (io["norm2_g"][0].rearrange("(j p) -> j p", p=P), 56, 8),
                            (io["c"][0].rearrange("(j p) -> j p", p=P), 64, 8),
                            (io["c_ctx"].rearrange("(j p) -> j p", p=P), 72, 8)]
                    for src, at, n in rows:
                        sp.dma_start(vecs[at:at + n, :], src).then_inc(a_vec, 16)
                    for n in range(GM * NK):
                        g, k = n // NK, n % NK
                        if n >= WR:
                            sp.wait_ge(a_wused, n - WR + 1)
                        sp.dma_start(wm[:, n % WR, :], io["w_mod"][0, k * P:(k + 1) * P, g * COLS:(g + 1) * COLS]
                                     ).then_inc(a_w[n % WR], 16)
                        for t in range(2 * n, min(2 * n + 2, T)):
                            sp.dma_start(x[:, t, :], x_rows(t)).then_inc(a_x[t], 16)
                    for k in range(NK):
                        row_tile(sp, 0, k, False, k)

                @block.tensor
                def _(pe):
                    pe.wait_ge(a_const, 16)
                    pe.wait_ge(a_vec, 5 * 16)
                    pe.transpose(vps, vecs[:], ident[0:80, 0:80]).then_inc(a_vt, 1)
                    pe.wait_ge(a_cond, 2)

                    def mod_rows(n):
                        g, k = n // NK, n % NK
                        if g and k == 0:
                            pe.wait_ge(a_row, g)
                        pe.wait_ge(a_w[n % WR], 16 * (n // WR + 1))
                        for q in range(4):
                            mm = pe.matmul(mod[:, q, :], cond[:, k, :], wm[:, n % WR, q * 512:(q + 1) * 512],
                                           start=(k == 0), stop=(k == NK - 1))
                        mm.then_inc(a_wused, 1)

                    def mod_columns(g):
                        pe.wait_ge(a_row, g + 1)
                        if g:
                            pe.wait_ge(a_mod, g)
                        for j in range(COLS // P):
                            mm = pe.transpose(mps[:, g * (COLS // P) + j, :], mrow[:, j * P:(j + 1) * P], ident[0:2, 0:2])
                        mm.then_inc(a_mt, 1)

                    def h_tiles(n):
                        k, g = groups[n]
                        if n >= 3:
                            pe.wait_ge(a_full, n - 2)
                        for q, t in enumerate(group_tiles(g)):
                            if k == 0:
                                pe.wait_ge(a_xn, t + 1)
                            mm = pe.transpose(tps[n % 3][:, q * P:(q + 1) * P], x[:, t, k * P:(k + 1) * P], ident[:])
                        mm.then_inc(a_tp, 1)

                    for n in range(NK):
                        mod_rows(n)
                    for m in range(NK):
                        for n in range(3 * m, 3 * m + 3):
                            h_tiles(n)
                        if m == 0:
                            mod_columns(0)
                        for n in range(NK + 2 * m, NK + 2 * m + 2):
                            mod_rows(n)
                        if m == NK // 2 - 1:
                            mod_columns(1)
                    mod_columns(2)

                @block.scalar
                def _(act):
                    act.sem_inc(b_hi, NG)
                    act.wait_ge(a_vtc, 1)
                    act.activation(cond[:, :, 0], vecT[:, 64:72], ACT.Silu).then_inc(a_cond, 1)
                    act.activation(cond[:, :, 1], vecT[:, 72:80], ACT.Silu).then_inc(a_cond, 1)
                    for t in range(T):
                        act.wait_ge(a_x[t], 16)
                        if t >= 2:
                            act.wait_ge(a_sq, t - 1)
                        act.activation(sq[:, t % 2, :], x[:, t, :], ACT.Square, accum_out=ssum[:, t:t + 1]).then_inc(a_sq, 1)

                    def take_rows(g):
                        act.wait_ge(a_wused, NK * (g + 1))
                        if g:
                            act.wait_ge(a_mt, g)
                        act.activation(mrow[:].rearrange("r (q c) -> r q c", q=4), mod[:], ACT.Copy).then_inc(a_row, 1)

                    take_rows(0)
                    for n, (k, g) in enumerate(groups):
                        a, b = 512 * g, min(512 * g + 512, N)
                        act.wait_ge(a_full, n + 1)
                        act.activation(hT[0][:, k, a:b], hfull[:, n % 2, 0:b - a], ACT.Copy).then_inc(a_hi, 1)
                        if n == 3 * NK // 2 - 1:
                            take_rows(1)
                    for k in range(NK):
                        qkv_hi(act, 0, k)
                    take_rows(2)

                @block.gpsimd
                def _(gp):
                    gp.memset(nhalf[:], -0.5).then_inc(a_half, 1)
                    gp.wait_ge(a_half, 1)
                    for n in range(2):
                        half = slice(n * T // 2, (n + 1) * T // 2)
                        gp.wait_ge(a_sq, half.stop)
                        gp.tensor_scalar(ssum[:, half], ssum[:, half], 1.0 / D, EPS, ALU.mult, ALU.add).then_inc(a_mean, 1)
                        gp.wait_ge(a_mean, n + 1)
                        gp.tensor_tensor(rstd[:, half], ssum[:, half], nhalf[:, half], ALU.pow).then_inc(a_rstd, 1)
                    for n, (k, g) in enumerate(groups):
                        a, b = 512 * g, min(512 * g + 512, N)
                        gp.wait_ge(a_hi, n + 1)
                        gp.tensor_tensor(hT[1][:, k, a:b], hfull[:, n % 2, 0:b - a], hT[0][:, k, a:b].bitcast(F32),
                                         ALU.subtract).then_inc(a_lo, 1)

                @block.vector
                def _(dve):
                    dve.sem_inc(b_lo, NG)
                    dve.wait_ge(a_vt, 1)
                    dve.tensor_copy(vecT[:], vps).then_inc(a_vtc, 1)
                    for t in range(T):
                        if t % (T // 2) == 0:
                            dve.wait_ge(a_rstd, t // (T // 2) + 1)
                        dve.tensor_scalar(x[:, t, :], x[:, t, :], rstd[:, t:t + 1], None, ALU.mult).then_inc(a_xn, 1)

                    def take_mod(g):
                        per = COLS // P
                        dve.wait_ge(a_mt, g + 1)
                        bm = vecT[:, per * g:per * (g + 1)].unsqueeze(2).broadcast_to([P, per, 2])
                        out = modT[:].rearrange("p a k r -> p (a k) r")[:, per * g:per * (g + 1), :]
                        dve.tensor_tensor(out, mps[:, per * g:per * (g + 1), :], bm, ALU.add).then_inc(a_mod, 1)
                        dve.wait_ge(a_mod, g + 1)

                    def take_scale(m):
                        gm = vecT[:, 48 + 8 * m:56 + 8 * m].unsqueeze(2).broadcast_to([P, NK, 2])
                        dve.scalar_tensor_tensor(scaleA[:, m, :, :], modT[:, 1 + 3 * m, :, :], 1.0, gm,
                                                 ALU.add, ALU.mult).then_inc(a_scale, 1)

                    dve.wait_ge(a_vtc, 1)
                    take_mod(0)
                    take_scale(0)
                    dve.wait_ge(a_scale, 1)
                    for n, (k, g) in enumerate(groups):
                        a, b = 512 * g, min(512 * g + 512, N)
                        r = 0 if g < 2 else 1
                        dve.wait_ge(a_tp, n + 1)
                        if n >= 2:
                            dve.wait_ge(a_lo, n - 1)
                        dve.tensor_scalar(hfull[:, n % 2, 0:b - a], tps[n % 3][:, 0:b - a],
                                          scaleA[:, 0, k, r:r + 1], modT[:, 0, k, r:r + 1],
                                          ALU.mult, ALU.add).then_inc(a_full, 1)
                        if n == 3 * NK // 2 + 2:
                            take_mod(1)
                    for k in range(NK):
                        qkv_lo(dve, 0, k)
                    take_mod(2)
                    take_scale(1)

        with ExitStack() as c:
            wg = [sb("wg_hi", [P, NK, 256], F32R, c), sb("wg_lo", [P, NK, 256], F32R, c)]
            p = sb("p", [P, T, 384], F32, c)
            AT = sb("AT", [P, T, 2, P], F32, c)
            qTd = sb("qTd", [P, T, 2, P], F32, c)
            S = sb("S", [P, T, 2, P], F32, c)
            rope = sb("rope", [P, TS, 2, P], F32, c)
            mask = sb("mask", [P, H, 2, P], F32, c)
            qdec = sb("qdec", [P, H, 2, P], F32, c)
            kdec = sb("kdec", [P, H, 2], F32, c)
            sdec = sb("sdec", [P, H, 2], F32, c)
            rt = sb("rt", [P, 2, 2, P], F32, c)
            qkT = sb("qkT", [P, 2, 2, P], F32, c)
            vdec = sb("vdec", [P, 2, 2, P], F32, c)
            fin = sb("fin", [P, 2, P], F32, c)
            stats = sb("stats", [P, 2, 2, 6], F32, c)
            mv = sb("mv", [P, 2, 2, 2], F32, c)
            var = sb("var", [P, 2, 2], F32, c)
            rs = sb("rs", [P, 2, 2], F32, c)
            z = sb("z", [P, 2, 2, P], F32, c)
            ysb = sb("ysb", [P, 2, P], F32, c)
            yT = sb("yT", [P, 2, P], F32, c)
            proj = [ps(f"proj{i}", [P, 512], c) for i in range(2)]
            tp = ps("tp", [P, 512], c)
            att = ps("att", [P, 512], c)
            ups = ps("ups", [P, 512], c)
            ops = [ps(f"ops{i}", [P, 512], c) for i in range(2)]
            yps = ps("yps", [P, 512], c)
            b_tab = sem("b_tab")
            b_proj = sem("b_proj")
            b_qkv = sem("b_qkv")
            b_rt, b_rope = sem("b_rt"), sem("b_rope")
            b_vdec, b_gate = sem("b_vdec"), sem("b_gate")
            b_tr, b_trc, b_qtd = sem("b_tr"), sem("b_trc"), sem("b_qtd")
            b_att, b_atm = sem("b_att"), sem("b_atm")
            b_u, b_ud = sem("b_u"), sem("b_ud")
            b_s0, b_sb, b_fin, b_finout = sem("b_s0"), sem("b_sb"), sem("b_fin"), sem("b_finout")
            b_o, b_st, b_mv, b_var, b_rs = sem("b_o"), sem("b_st"), sem("b_mv"), sem("b_var"), sem("b_rs")
            b_z, b_zg, b_y = sem("b_z"), sem("b_zg"), sem("b_y")
            b_yt, b_yc = sem("b_yt"), sem("b_yc")
            b_yout = [sem("b_yout0"), sem("b_yout1")]

            nc.clear_and_free_semaphores([sm for sm in sems if sm.name.startswith("a_") and sm not in (a_const, *a_x)])
            state_in, state_out = io["state_ret"], io["state_out"]
            ORDER = [9, 8] + list(range(TS - 1, -1, -1))

            def heads(eng, body):
                with eng.Fori(0, H - 1) as h:
                    body(h, False)
                body(H - 1, True)

            with nc.Block() as block:
                @block.sync
                def _(sp):
                    for dst, src in ((mask, "c_mask"), (qdec, "c_qdec"), (kdec, "c_kdec"), (sdec, "c_sdec")):
                        sp.dma_start(dst[:], io[src]).then_inc(b_tab, 16)
                    sp.dma_start(rope[:], io["c_rope"].rearrange("(t p) a c -> p t a c", p=P)).then_inc(b_tab, 16)
                    for sm in b_yout:
                        sp.sem_inc(sm, 16)
                    sp.sem_inc(b_finout, 32)

                    def first_states(h):
                        for d, at in ((0, 0), (1, TS - 1)):
                            src = state_in[0, 0, d, bass.ds(h, 1), :, :].rearrange("a p e -> p (a e)")
                            sp.dma_start(S[:, at, d, :], src).then_inc(b_s0, 16)

                    first_states(0)

                    def body(h, last):
                        for k in range(NK):
                            row_tile(sp, h, k, True, NK + 2 * NK * h + k)
                        for g in range(T + 4):
                            if g < NK and not last:
                                row_tile(sp, h + 1, g, False, 2 * NK * (h + 1) + g)
                            if g == 4:
                                sp.wait_ge(b_fin, h + 1)
                                for d in range(2):
                                    dst = state_out[0, 0, d, bass.ds(h, 1), :, :].rearrange("a p e -> p (a e)")
                                    sp.dma_start(dst, fin[:, d, :]).then_inc(b_finout, 16)
                            if g >= 4:
                                j = g - 4
                                t = ORDER[j]
                                waits(sp, (b_yc, 1 + T * h + j + 1))
                                dst = catT[bass.ds((H + h) * P, P), t * P:(t + 1) * P]
                                sp.dma_start(dst, yT[:, j % 2, :]).then_inc(b_yout[j % 2], 16)
                        if not last:
                            sp.wait_ge(b_o, T * (h + 1))
                            first_states(h + 1)

                    heads(sp, body)
                    for sm in b_yout:
                        sp.wait_ge(sm, 16 + 16 * H * T // 2)
                    sp.wait_ge(b_finout, 32 + 32 * H)

                @block.tensor
                def _(pe):
                    pe.wait_ge(a_const, 16)
                    for sm, n in ((b_att, 2), (b_u, 2), (b_yt, 2)):
                        pe.sem_inc(sm, n)

                    def project(t, use, w, cols):
                        for k in range(NK):
                            for a, b in ((0, 0), (0, 1), (1, 0)):
                                mm = pe.matmul(proj[use % 2][:, 0:cols], hT[a][:, k, t * P:(t + 1) * P], w[b][:, k, :],
                                               start=(k == 0 and a == b), stop=(k == NK - 1 and a == 1))
                        mm.then_inc(b_proj, 1)

                    def body(h, last):
                        for s in range(T + 2):
                            if s < T:
                                if s == 0:
                                    pe.wait_ge(b_hi, NG + 2 * NK * h + NK)
                                    pe.wait_ge(b_lo, NG + 2 * NK * h + NK)
                                if s >= 2:
                                    pe.wait_ge(b_qkv, T * h + s - 1)
                                else:
                                    pe.wait_ge(b_gate, T * h + s + 1)
                                project(s, s, wq, 384)
                            if 1 <= s <= T:
                                t = s - 1
                                if t < TS:
                                    pe.wait_ge(b_rope, 1 + TS * h + t + 1)
                                else:
                                    pe.wait_ge(b_qkv, T * h + t + 1)
                                pe.wait_ge(b_trc, T * h + t + 1)
                                pe.transpose(tp[:, 0:P], p[:, t, 0:P], ident[:])
                                pe.transpose(tp[:, P:2 * P], p[:, t, P:2 * P], ident[:]).then_inc(b_tr, 1)
                                pe.wait_ge(b_vdec, T * h + t + 1)
                                pe.wait_ge(b_ud, T * h + t + 1)
                                pe.matmul(ups[:, 0:2 * P], p[:, t, P:2 * P], vdec[:, t % 2, :, :],
                                          start=True, stop=True).then_inc(b_u, 1)
                            if s >= 2:
                                t = s - 2
                                pe.wait_ge(b_trc, 1 + T * h + t + 1)
                                pe.wait_ge(b_atm, T * h + t + 1)
                                pe.matmul(att[:, 0:P], qkT[:, t % 2, 1, :], qkT[:, t % 2, 0, :],
                                          start=True, stop=True).then_inc(b_att, 1)
                        for g in range(T + 3):
                            if g < T:
                                if g == 0:
                                    pe.wait_ge(b_hi, NG + 2 * NK * h + 2 * NK)
                                    pe.wait_ge(b_lo, NG + 2 * NK * h + 2 * NK)
                                if g < 2:
                                    pe.wait_ge(b_qkv, T * h + T - 1 + g)
                                else:
                                    pe.wait_ge(b_gate, 2 + T * h + g - 1)
                                project(ORDER[g], g, wg, 256)
                                t = ORDER[g]
                                if g == 0:
                                    pe.wait_ge(b_atm, 1 + T * h + T)
                                    pe.wait_ge(b_qtd, 2 + T * h + T)
                                    pe.wait_ge(b_ud, 1 + T * h + T)
                                if t < TS - 1:
                                    pe.wait_ge(b_sb, (TS - 1) * h + TS - 1 - t)
                                pe.wait_ge(b_z, T * h + g + 1)
                                for d in range(2):
                                    alone = (t, d) in ((TS, 0), (T - 1, 1))
                                    mm = pe.matmul(ops[g % 2][:, d * P:(d + 1) * P], AT[:, t, d, :],
                                                   p[:, t, 2 * P:3 * P], start=True, stop=alone)
                                    if not alone:
                                        mm = pe.matmul(ops[g % 2][:, d * P:(d + 1) * P], qTd[:, t, d, :],
                                                       S[:, t, d, :], start=False, stop=True)
                                mm.then_inc(b_o, 1)
                            if g >= 3:
                                j = g - 3
                                pe.wait_ge(b_y, 2 + T * h + j + 1)
                                pe.wait_ge(b_yc, T * h + j + 1)
                                pe.transpose(yps[:, 0:P], ysb[:, j % 2, :], ident[:]).then_inc(b_yt, 1)

                    heads(pe, body)

                @block.scalar
                def _(act):
                    for sm, n in ((b_gate, 2), (b_trc, 1), (b_yc, 1)):
                        act.sem_inc(sm, n)

                    def gates_hi(h, k):
                        act.wait_ge(b_raw[k % NG], 16 * (4 * h + 2 + k // NG + 1))
                        act.activation(wg[0][:, k, :], raw[:, k % NG, 0:256], ACT.Copy).then_inc(b_hi, 1)

                    act.wait_ge(b_tab, 5 * 16)

                    def body(h, last):
                        for s in range(T + 1):
                            if s < T:
                                act.wait_ge(b_proj, 2 * T * h + s + 1)
                                act.activation(p[:, s, :], proj[s % 2][:, 0:3 * P], ACT.Copy).then_inc(b_qkv, 1)
                                waits(act, (b_qkv, T * h + s + 1), (b_u, T * h + s + 1))
                                for d in range(2):
                                    op = act.activation(vdec[:, s % 2, d, :], p[:, s, 2 * P:3 * P], ACT.Copy,
                                                        scale=kdec[:, bass.ds(h, 1), d])
                                op.then_inc(b_vdec, 1)
                            if s < NK:
                                gates_hi(h, s)
                            if s >= 1:
                                t = s - 1
                                act.wait_ge(b_tr, T * h + t + 1)
                                act.wait_ge(b_att, T * h + t + 1)
                                act.wait_ge(b_qtd, T * h + t + 1)
                                act.activation(qkT[:, t % 2, :, :].rearrange("p a c -> p (a c)"), tp[:, 0:2 * P],
                                               ACT.Copy).then_inc(b_trc, 1)
                        for g in range(T + 3):
                            if g < T:
                                act.wait_ge(b_proj, 2 * T * h + T + g + 1)
                                act.wait_ge(b_zg, T * h + g + 1)
                                act.activation(p[:, ORDER[g], 0:2 * P], proj[g % 2][:, 0:2 * P],
                                               ACT.Silu).then_inc(b_gate, 1)
                            if g < NK and not last:
                                qkv_hi(act, h + 1, g)
                            if g >= 3:
                                j = g - 3
                                act.wait_ge(b_yt, 2 + T * h + j + 1)
                                act.wait_ge(b_yout[j % 2], 16 * (T // 2 * h + j // 2 + 1))
                                act.activation(yT[:, j % 2, :], yps[:, 0:P], ACT.Copy).then_inc(b_yc, 1)

                    heads(act, body)

                @block.vector
                def _(dve):
                    for sm, n in ((b_ud, 1), (b_atm, 1), (b_z, 2)):
                        dve.sem_inc(sm, n)

                    def gates_lo(h, k):
                        dve.wait_ge(b_hi, NG + 2 * NK * h + NK + k + 1)
                        dve.tensor_tensor(wg[1][:, k, :], raw[:, k % NG, 0:256], wg[0][:, k, :].bitcast(F32),
                                          ALU.subtract).then_inc(b_lo, 1)

                    dve.wait_ge(b_tab, 5 * 16)

                    def body(h, last):
                        sd = [sdec[:, bass.ds(h, 1), d] for d in range(2)]
                        for s in range(T + 2):
                            if s < TS:
                                dve.wait_ge(b_qkv, T * h + s + 1)
                                dve.wait_ge(b_rope, TS * h + s + 1)
                                qk = p[:, s, 0:2 * P].rearrange("p (z c) -> p z c", z=2)
                                for a in range(2):
                                    tab = rope[:, s, a, :].unsqueeze(1).broadcast_to([P, 2, P])
                                    op = dve.tensor_tensor(rt[:, a, :, :], qk, tab, ALU.mult)
                                op.then_inc(b_rt, 1)
                            if s < NK:
                                gates_lo(h, s)
                            if 1 <= s <= T:
                                t = s - 1
                                dve.wait_ge(b_u, 2 + T * h + t + 1)
                                dve.wait_ge(b_ud, 1 + T * h + t)
                                if t == 0:
                                    dve.wait_ge(b_s0, 32 * h + 32)
                                uf, ub = ups[:, 0:P], ups[:, P:2 * P]
                                if t < TS - 1:
                                    op = dve.scalar_tensor_tensor(S[:, t + 1, 0, :], S[:, t, 0, :], sd[0], uf,
                                                                  ALU.mult, ALU.add)
                                if 1 <= t < TS:
                                    op = dve.tensor_copy(S[:, t - 1, 1, :], ub)
                                if t == TS:
                                    dve.tensor_copy(S[:, t + 1, 0, :], uf)
                                    dve.wait_ge(b_finout, 32 * h + 32)
                                    op = dve.tensor_copy(fin[:, 1, :], ub)
                                if t == TS + 1:
                                    dve.scalar_tensor_tensor(fin[:, 0, :], S[:, t, 0, :], sd[0], uf, ALU.mult, ALU.add)
                                    dve.scalar_tensor_tensor(fin[:, 1, :], ub, sd[1], fin[:, 1, :],
                                                             ALU.mult, ALU.add).then_inc(b_fin, 1)
                                    op = dve.tensor_copy(S[:, t - 1, 1, :], ub)
                                op.then_inc(b_ud, 1)
                            if s >= 2:
                                t = s - 2
                                dve.wait_ge(b_att, 2 + T * h + t + 1)
                                m = mask[:, bass.ds(h, 1), :, :].rearrange("p a d c -> p (a d) c")
                                dve.tensor_tensor(AT[:, t, :, :], att[:, 0:P].unsqueeze(1).broadcast_to([P, 2, P]), m,
                                                  ALU.mult).then_inc(b_atm, 1)
                        dve.wait_ge(b_ud, 1 + T * h + T)
                        for n in range(TS - 1):
                            t = TS - 1 - n
                            if n:
                                dve.wait_ge(b_sb, (TS - 1) * h + n)
                            dve.scalar_tensor_tensor(S[:, t - 1, 1, :], S[:, t, 1, :], sd[1], S[:, t - 1, 1, :],
                                                     ALU.mult, ALU.add).then_inc(b_sb, 1)
                        for j in range(T + 1):
                            if j < T:
                                dve.wait_ge(b_o, T * h + j + 1)
                                for d in range(2):
                                    op = dve.bn_stats(stats[:, j % 2, d, :], ops[j % 2][:, d * P:(d + 1) * P])
                                op.then_inc(b_st, 1)
                                waits(dve, (b_st, T * h + j + 1))
                                for d in range(2):
                                    op = dve.bn_aggr(mv[:, j % 2, d, :], stats[:, j % 2, d, :])
                                op.then_inc(b_mv, 1)
                            if j < NK and not last:
                                qkv_lo(dve, h + 1, j)
                            if j >= 1:
                                i = j - 1
                                dve.wait_ge(b_rs, T * h + i + 1)
                                dve.wait_ge(b_y, T * h + i + 1)
                                for d in range(2):
                                    op = dve.tensor_scalar(z[:, i % 2, d, :], ops[i % 2][:, d * P:(d + 1) * P],
                                                           mv[:, i % 2, d, 0:1], rs[:, i % 2, d:d + 1],
                                                           ALU.subtract, ALU.mult)
                                op.then_inc(b_z, 1)

                    heads(dve, body)

                @block.gpsimd
                def _(gp):
                    for sm, n in ((b_rope, 1), (b_qtd, 2), (b_zg, T), (b_y, 2)):
                        gp.sem_inc(sm, n)
                    gp.wait_ge(b_tab, 5 * 16)

                    def body(h, last):
                        for s in range(T + 1):
                            if s < TS:
                                gp.wait_ge(b_rt, TS * h + s + 1)
                                cs = rt[:, 0, :, :].rearrange("p z (a s w) -> p (z a) s w", a=2, s=2)
                                sn = rt[:, 1, :, :].rearrange("p z (a s w) -> p (z a) s w", a=2, s=2)
                                out = p[:, s, 0:2 * P].rearrange("p (z s w) -> p z s w", s=2, w=32)
                                gp.tensor_tensor(out[:, :, 0, :], cs[:, :, 0, :], sn[:, :, 1, :], ALU.subtract)
                                gp.tensor_tensor(out[:, :, 1, :], cs[:, :, 1, :], sn[:, :, 0, :],
                                                 ALU.add).then_inc(b_rope, 1)
                            if s >= 1:
                                t = s - 1
                                waits(gp, (b_trc, 1 + T * h + t + 1))
                                qd = qdec[:, bass.ds(h, 1), :, :].rearrange("p a d c -> p (a d) c")
                                gp.tensor_tensor(qTd[:, t, :, :], qkT[:, t % 2, 0, :].unsqueeze(1).broadcast_to([P, 2, P]),
                                                 qd, ALU.mult).then_inc(b_qtd, 1)
                        for j in range(T + 1):
                            if j < T:
                                waits(gp, (b_mv, T * h + j + 1))
                                gp.tensor_scalar(var[:, j % 2, :], mv[:, j % 2, :, 1], EPS, None, ALU.add).then_inc(b_var, 1)
                                gp.wait_ge(b_var, T * h + j + 1)
                                gp.tensor_tensor(rs[:, j % 2, :], var[:, j % 2, :], nhalf[:, 0:2], ALU.pow).then_inc(b_rs, 1)
                            if j >= 1:
                                i = j - 1
                                gp.wait_ge(b_z, 2 + T * h + i + 1)
                                gp.wait_ge(b_gate, 2 + T * h + i + 1)
                                zi = z[:, i % 2, :, :].rearrange("p d c -> p (d c)")
                                gp.tensor_tensor(zi, zi, p[:, ORDER[i], 0:2 * P], ALU.mult).then_inc(b_zg, 1)
                                gp.wait_ge(b_zg, T + T * h + i + 1)
                                gp.wait_ge(b_yt, T * h + i + 1)
                                gp.tensor_tensor(ysb[:, i % 2, :], z[:, i % 2, 0, :], z[:, i % 2, 1, :],
                                                 ALU.add).then_inc(b_y, 1)

                    heads(gp, body)

        stack_w.close()

        with ExitStack() as c:
            raw = sb("rawC", [P, NK, P], F32, c)
            w = [sb("wf_hi", [P, NK, P], F32R, c), sb("wf_lo", [P, NK, P], F32R, c)]
            chan = sb("chan", [P, 2, P], F32, c)
            wmix = sb("wmix", [P, H, P], F32, c)
            M = sb("M", [P, H, 2, P], F32, c)
            pcos = sb("pcos", [P, 4, 513], F32, c)
            palt = sb("palt", [1, 513], F32, c)
            psin = sb("psin", [P, 4, 512], F32, c)
            cdft = sb("cdft", [P, 2, 2, N_P], F32, c)
            UT = sb("UT", [P, N], F32, c)
            Ue = sb("Ue", [P, 513], F32, c)
            Uo = sb("Uo", [P, 512], F32, c)
            Z = sb("Z", [P, 6, 2, P], F32, c)
            Zrow = sb("Zrow", [1, P], F32, c)
            Bs = sb("Bs", [P, 512], F32, c)
            yf = sb("yf", [P, N], F32, c)
            up = [ps(f"up{i}", [P, 512], c) for i in range(3)]
            zp = [ps(f"zp{i}", [P, 512], c) for i in range(2)]
            pa, pb, pm = ps("pa", [P, 512], c), ps("pb", [P, 512], c), ps("pm", [P, 512], c)
            c_tab, c_dft, c_raw = sem("c_tab"), sem("c_dft"), sem("c_raw")
            c_hi, c_lo, c_m, c_mc = sem("c_hi"), sem("c_lo"), sem("c_m"), sem("c_mc")
            c_up, c_ut = sem("c_up"), sem("c_ut")
            c_fold, c_z, c_za, c_zd = sem("c_fold"), sem("c_z"), sem("c_za"), sem("c_zd")
            c_row, c_rowc = sem("c_row"), sem("c_rowc")
            c_pos, c_bs, c_yd, c_ya, c_out = sem("c_pos"), sem("c_bs"), sem("c_yd"), sem("c_ya"), sem("c_out")
            w_in = io["w_in"][0].rearrange("(k p) c -> p k c", p=P)
            token_groups = [(0, 512), (512, 1024), (1024, 1280)]

            def over_groups(eng, body):
                body(0, True, False)
                with eng.Fori(1, H - 1) as g:
                    body(g, False, False)
                body(H - 1, False, True)

            with nc.Block() as block:
                @block.sync
                def _(sp):
                    sp.sem_inc(c_out, 16)

                    def weights(g):
                        sp.dma_start(raw[:], w_in[:, :, bass.ds(g * P, P)]).then_inc(c_raw, 16)

                    def store(g):
                        sp.wait_ge(c_yd, 1 + g + 1)
                        sp.wait_ge(c_ya, 1 + g + 1)
                        sp.dma_start(catT[bass.ds(g * P, P), :], yf[:]).then_inc(c_out, 16)

                    weights(0)
                    sp.dma_start(chan[:], io["c_chan"]).then_inc(c_tab, 16)
                    sp.dma_start(wmix[:], io["w_fmix"][0].rearrange("g w v -> w g v")).then_inc(c_tab, 16)
                    sp.dma_start(pcos[:], io["c_poscos"][0:512, :].rearrange("(t p) k -> p t k", p=P)).then_inc(c_dft, 16)
                    sp.dma_start(palt[:], io["c_poscos"][512:513, :]).then_inc(c_dft, 16)
                    sp.dma_start(psin[:], io["c_possin"].rearrange("(t p) k -> p t k", p=P)).then_inc(c_dft, 16)
                    sp.dma_start(cdft[:], io["c_ctxdft"].rearrange("(t p) a k -> p t a k", p=P)).then_inc(c_dft, 16)

                    def body(g, first, last):
                        if not last:
                            sp.wait_ge(c_lo, 2 * g + 2)
                            weights(g + 1)
                        if not first:
                            store(g - 1)

                    over_groups(sp, body)
                    store(H - 1)
                    sp.wait_ge(c_out, 16 + 16 * H)

                @block.tensor
                def _(pe):
                    def project(g):
                        pe.wait_ge(c_lo, 2 * g + 1)
                        for q, (a, b) in enumerate(token_groups):
                            pe.wait_ge(c_ut, 3 * g + q + 1)
                            for k in range(NK):
                                if q == 0 and k == NK // 2:
                                    pe.wait_ge(c_lo, 2 * g + 2)
                                for i, j in ((0, 0), (0, 1), (1, 0)):
                                    mm = pe.matmul(up[q][:, 0:b - a], w[i][:, k, :], hT[j][:, k, a:b],
                                                   start=(k == 0 and i == j), stop=(k == NK - 1 and i == 1))
                            mm.then_inc(c_up, 1)

                    def mix(g):
                        m = M[:, bass.ds(g, 1), :, :].rearrange("p g a v -> p (g a) v")
                        pe.wait_ge(c_fold, g + 1)
                        for n in range(6):
                            pe.wait_ge((c_za, c_zd)[n % 2], 3 * g + n // 2 + 1)
                            if n < 4:
                                pe.matmul(zp[n % 2][:, 0:P], Ue[:, n * P:(n + 1) * P], m[:, 0, :], start=True, stop=True)
                                mm = pe.matmul(zp[n % 2][:, P:2 * P], Uo[:, n * P:(n + 1) * P], m[:, 1, :],
                                               start=True, stop=True)
                            else:
                                t = TS + n - 4
                                mm = pe.matmul(zp[n % 2][:, 0:2 * P], UT[:, t * P:(t + 1) * P], m, start=True, stop=True)
                            mm.then_inc(c_z, 1)
                            if n == 3:
                                waits(pe, (c_yd, g + 1), (c_ya, g + 1))
                                pe.matmul(pm[0:1, 384:512], Ue[:, 512:513], m[:, 0, :], start=True,
                                          stop=True).then_inc(c_row, 1)
                        for n in range(4):
                            pe.wait_ge((c_za, c_zd)[n % 2], 1 + 3 * g + n // 2 + 1)
                            pe.matmul(pa[:], Z[:, n, 0, :], pcos[:, n, 0:512], start=(n == 0), stop=False)
                            pe.matmul(pb[:], Z[:, n, 1, :], psin[:, n, :], start=(n == 0), stop=(n == 3))
                        pe.wait_ge(c_rowc, g + 1)
                        pe.matmul(pa[:], Zrow[:], palt[:, 0:512], start=False, stop=True)
                        for n in range(4):
                            pe.matmul(pm[:, 256:257], Z[:, n, 0, :], pcos[:, n, 512:513], start=(n == 0), stop=False)
                        pe.matmul(pm[:, 256:257], Zrow[:], palt[:, 512:513], start=False, stop=True)
                        pe.wait_ge(c_za, 1 + 3 * g + 3)
                        pe.wait_ge(c_zd, 1 + 3 * g + 3)
                        for n in range(2):
                            for a in range(2):
                                mm = pe.matmul(pm[:, 0:N_P], Z[:, 4 + n, a, :], cdft[:, n, a, :],
                                               start=(n + a == 0), stop=(n + a == 2))
                        mm.then_inc(c_pos, 1)

                    pe.wait_ge(c_tab, 2 * 16)
                    for g in range(H):
                        for a in range(2):
                            mm = pe.matmul(zp[g // 2][:, (g % 2 * 2 + a) * P:(g % 2 * 2 + a + 1) * P], chan[:, a, :],
                                           wmix[:, g, :], start=True, stop=True)
                        mm.then_inc(c_m, 1)
                    project(0)
                    pe.wait_ge(c_mc, 2)
                    pe.wait_ge(c_dft, 4 * 16)
                    with pe.Fori(0, H - 1) as g:
                        project(g + 1)
                        mix(g)
                    mix(H - 1)

                def copy_z(eng, fn, g, n, done):
                    eng.wait_ge(c_z, 6 * g + n + 1)
                    fn(Z[:, n, :, :].rearrange("p a v -> p (a v)"), zp[n % 2][:, 0:2 * P]).then_inc(done, 1)

                @block.scalar
                def _(act):
                    for sm, n in ((c_ut, 3), (c_za, 1), (c_ya, 1)):
                        act.sem_inc(sm, n)

                    def split_hi(g):
                        act.wait_ge(c_raw, 16 * (g + 1))
                        if not isinstance(g, int) or g:
                            act.wait_ge(c_up, 3 * g)
                        for half in (slice(0, NK // 2), slice(NK // 2, NK)):
                            act.activation(w[0][:, half, :], raw[:, half, :], ACT.Copy).then_inc(c_hi, 1)

                    def take_u(g):
                        for q, (a, b) in enumerate(token_groups):
                            act.wait_ge(c_up, 3 * g + q + 1)
                            act.activation(UT[:, a:b], up[q][:, 0:b - a], ACT.Copy).then_inc(c_ut, 1)

                    def tiles(g):
                        for n in (0, 2, 4):
                            copy_z(act, lambda o, i: act.activation(o, i, ACT.Copy), g, n, c_za)
                            if n == 2:
                                act.wait_ge(c_row, g + 1)
                                act.activation(Zrow[:], pm[0:1, 384:512], ACT.Copy).then_inc(c_rowc, 1)

                    def finish(g):
                        act.wait_ge(c_pos, g + 1)
                        act.activation(Bs[:], pb[:], ACT.Copy).then_inc(c_bs, 1)
                        act.wait_ge(c_out, 16 * (g + 1))
                        act.activation(yf[:, 512:513], pm[:, 256:257], ACT.Copy)
                        act.activation(yf[:, N_S:N], pm[:, 0:N_P], ACT.Copy).then_inc(c_ya, 1)

                    split_hi(0)
                    for i in range(2):
                        act.wait_ge(c_m, 2 * i + 2)
                        act.activation(M[:, 2 * i:2 * i + 2, :, :].rearrange("p g a v -> p (g a v)"), zp[i][:],
                                       ACT.Copy).then_inc(c_mc, 1)
                    take_u(0)

                    def body(g, first, last):
                        if not last:
                            split_hi(g + 1)
                        if not first:
                            finish(g - 1)
                        tiles(g)
                        if not last:
                            act.wait_ge(c_fold, g + 1)
                            act.wait_ge(c_z, 6 * g + 6)
                            take_u(g + 1)

                    over_groups(act, body)
                    finish(H - 1)

                @block.vector
                def _(dve):
                    for sm, n in ((c_zd, 1), (c_yd, 1)):
                        dve.sem_inc(sm, n)

                    def split_lo(g):
                        for n, half in enumerate((slice(0, NK // 2), slice(NK // 2, NK))):
                            dve.wait_ge(c_hi, 2 * g + n + 1)
                            dve.tensor_tensor(w[1][:, half, :], raw[:, half, :], w[0][:, half, :].bitcast(F32),
                                              ALU.subtract).then_inc(c_lo, 1)

                    def fold(g):
                        dve.wait_ge(c_ut, 3 + 3 * g + 2)
                        back = UT[:, 1023:512:-1]
                        dve.tensor_tensor(Ue[:, 1:512], UT[:, 1:512], back, ALU.add)
                        dve.tensor_tensor(Uo[:, 1:512], UT[:, 1:512], back, ALU.subtract)
                        dve.tensor_copy(Ue[:, 0:513:512], UT[:, 0:513:512]).then_inc(c_fold, 1)

                    def tiles(g):
                        for n in (1, 3, 5):
                            copy_z(dve, dve.tensor_copy, g, n, c_zd)

                    def finish(g):
                        dve.wait_ge(c_bs, g + 1)
                        dve.wait_ge(c_out, 16 * (g + 1))
                        dve.tensor_tensor(yf[:, 0:512], pa[:], Bs[:], ALU.add)
                        dve.tensor_tensor(yf[:, 1023:512:-1], pa[:, 1:512], Bs[:, 1:512], ALU.subtract).then_inc(c_yd, 1)

                    dve.memset(Uo[:, 0:1], 0.0)
                    split_lo(0)
                    fold(0)

                    def body(g, first, last):
                        if not last:
                            split_lo(g + 1)
                        if not first:
                            finish(g - 1)
                        tiles(g)
                        if not last:
                            dve.wait_ge(c_row, g + 1)
                            fold(g + 1)

                    over_groups(dve, body)
                    finish(H - 1)
        stack_h.close()

        L = sb("L", [P, T, E])
        gates = [sb("gate1", [P, 2, D]), sb("gate2", [P, 2, D])]
        with ExitStack() as c:
            rawo = sb("rawo", [P, NK, D], F32, c)
            wo = [sb("wo_hi", [P, NK, D], F32R, c), sb("wo_lo", [P, NK, D], F32R, c)]
            ones = sb("ones", [P, P], F32, c)
            diag = sb("diag", [P, 2, NK, P], F32, c)
            rawc = sb("rawc", [P, 2, NK, P], F32, c)
            ca = [sb("cat_hi", [P, 2, NK, P], F32R, c), sb("cat_lo", [P, 2, NK, P], F32R, c)]
            xt = sb("xt", [P, 2, D], F32, c)
            x1 = sb("x1", [P, 2, D], F32, c)
            xn = sb("xn", [P, 2, D], F32, c)
            h2T = sb("h2T", [P, 2, NK, P], F32, c)
            sq = sb("sqD", [P, D], F32, c)
            ss = sb("ss", [P, 2, 1], F32, c)
            rs = sb("rsD", [P, 2, 1], F32, c)
            wr = sb("wr", [P, NK, E], F32, c)
            ops = [ps(f"opsD{i}", [P, 1024], c) for i in range(2)]
            trs = ps("trs", [P, 1024], c)
            rows = [ops[1], trs]
            lg = ps("lg", [P, 512], c)
            d_raw = [sem(f"d_raw{i}") for i in range(NK)]
            d_wr, d_cat, d_x = sem("d_wr"), [sem("d_cat0"), sem("d_cat1")], [sem("d_res0"), sem("d_res1")]
            d_hi, d_lo, d_ones, d_diag, d_bc, d_bcc = (sem("d_hi"), sem("d_lo"), sem("d_ones"), sem("d_diag"),
                                                       sem("d_bc"), sem("d_bcc"))
            d_chi, d_clo = sem("d_chi"), sem("d_clo")
            d_mm, d_gx, d_x1 = sem("d_mm"), sem("d_gx"), sem("d_x1")
            d_sq, d_ms, d_rs, d_xn = sem("d_sq"), sem("d_ms"), sem("d_rs"), sem("d_xn")
            d_st = [sem("d_st0"), sem("d_st1")]
            d_tr, d_h2, d_lg, d_lc = sem("d_tr"), sem("d_h2"), sem("d_lg"), sem("d_lc")
            catv = catT.rearrange("(k p) n -> p k n", p=P)

            def schedule(eng, step):
                for n in range(4):
                    step(n, n % 2)
                with eng.Fori(2, 4) as i:
                    step(2 * i, 0)
                    step(2 * i + 1, 1)
                for n in range(8, T + 3):
                    step(n, n % 2)

            def inside(n, m):
                return 0 <= n + m < T if isinstance(n, int) else True

            def group(n, m):
                return req(n + m) if isinstance(n, int) else 0

            with nc.Block() as block:
                @block.sync
                def _(sp):
                    for sm in d_st:
                        sp.sem_inc(sm, 32)
                    for k in range(NK):
                        if k < 2:
                            sp.dma_start(rawc[:, k, :, :], catv[:, :, k * P:(k + 1) * P]).then_inc(d_cat[k], 16)
                        sp.dma_start(rawo[:, k, :], io["w_out"][0, k * P:(k + 1) * P, :]).then_inc(d_raw[k], 16)
                    sp.dma_start(wr[:], io["w_router"][0].rearrange("(k p) e -> p k e", p=P)).then_inc(d_wr, 16)

                    def step(n, slot):
                        if inside(n, 0):
                            if not isinstance(n, int) or n >= 2:
                                sp.wait_ge(d_x1, n - 1)
                            if isinstance(n, int) and n >= TS:
                                src = io["x_prompt"][0, (n - TS) * P:(n - TS + 1) * P, :]
                            else:
                                src = io["x_sample"][0, bass.ds(n * P, P), :]
                            sp.dma_start(xt[:, slot, :], src).then_inc(d_x[slot], 16)
                        if inside(n, 2) and (not isinstance(n, int)):
                            sp.wait_ge(d_clo, 2 + n + 1)
                            sp.dma_start(rawc[:, slot, :, :], catv[:, :, bass.ds((n + 2) * P, P)]).then_inc(d_cat[slot], 16)
                        elif inside(n, 2):
                            sp.wait_ge(d_clo, 2 + n + 1)
                            sp.dma_start(rawc[:, slot, :, :], catv[:, :, (n + 2) * P:(n + 3) * P]).then_inc(d_cat[slot], 16)
                        if inside(n, -1):
                            sp.wait_ge(d_xn, n)
                            for dst, src in ((acc, x1), (xn2, xn)):
                                sp.dma_start(dst[bass.ds((n - 1) * P, P), :], src[:, 1 - slot, :]).then_inc(d_st[1 - slot], 16)

                    schedule(sp, step)
                    for sm in d_st:
                        sp.wait_ge(sm, 32 + 32 * T // 2)

                @block.tensor
                def _(pe):
                    pe.sem_inc(d_mm, 2)
                    pe.sem_inc(d_tr, 2)
                    pe.sem_inc(d_lg, 2)
                    pe.wait_ge(d_ones, 1)

                    def gate_rows(r):
                        pe.wait_ge(d_diag, r + 1)
                        for k in range(NK):
                            mm = pe.matmul(rows[r][:, k * P:(k + 1) * P], ones[:], diag[:, r, k, :], start=True, stop=True)
                        mm.then_inc(d_bc, 1)

                    def step(n, slot):
                        if inside(n, 0):
                            pe.wait_ge(d_clo, 2 + n + 1)
                            pe.wait_ge(d_gx, n + 1)
                            if isinstance(n, int) and n == 1:
                                pe.wait_ge(d_bcc, 1)
                            for k in range(NK):
                                if isinstance(n, int) and n == 0:
                                    pe.wait_ge(d_lo, k + 1)
                                for half in range(2):
                                    for a, b in ((0, 0), (0, 1), (1, 0)):
                                        mm = pe.matmul(ops[slot][:, half * 512:(half + 1) * 512], ca[a][:, slot, k, :],
                                                       wo[b][:, k, half * 512:(half + 1) * 512],
                                                       start=(k == 0 and a == b), stop=(k == NK - 1 and a == 1))
                                if isinstance(n, int) and n == 0 and k in (5, 7):
                                    gate_rows(k // 6)
                            mm.then_inc(d_mm, 1)
                        if inside(n, -3):
                            t = n - 3
                            if isinstance(n, int) and t == 0:
                                pe.wait_ge(d_wr, 16)
                            pe.wait_ge(d_h2, 1 + t + 1)
                            pe.wait_ge(d_lc, t + 1)
                            for k in range(NK):
                                mm = pe.matmul(lg[:, 0:E], h2T[:, 1 - slot, k, :], wr[:, k, :], start=(k == 0),
                                               stop=(k == NK - 1))
                            mm.then_inc(d_lg, 1)
                        if inside(n, -2):
                            t = n - 2
                            pe.wait_ge(d_xn, t + 1)
                            pe.wait_ge(d_h2, t + 1)
                            if isinstance(n, int) and t == 0:
                                pe.wait_ge(d_bcc, 2)
                            for k in range(NK):
                                mm = pe.transpose(trs[:, k * P:(k + 1) * P], xn[:, slot, k * P:(k + 1) * P], ident[:])
                            mm.then_inc(d_tr, 1)

                    schedule(pe, step)

                @block.scalar
                def _(act):
                    for sm, n in ((d_chi, 2), (d_h2, 1), (d_lc, 1)):
                        act.sem_inc(sm, n)
                    def split(m, slot):
                        act.wait_ge(d_cat[slot], 8 * (m - slot) + 16)
                        act.wait_ge(d_mm, m + 1)
                        act.activation(ca[0][:, slot, :, :], rawc[:, slot, :, :], ACT.Copy).then_inc(d_chi, 1)

                    split(0, 0)
                    for k in range(NK):
                        act.wait_ge(d_raw[k], 16)
                        act.activation(wo[0][:, k, :], rawo[:, k, :], ACT.Copy).then_inc(d_hi, 1)

                    def take_gate_row(r):
                        act.wait_ge(d_bc, r + 1)
                        act.activation(gates[0][:, r, :], rows[r][:], ACT.Copy).then_inc(d_bcc, 1)

                    take_gate_row(0)

                    def step(n, slot):
                        if inside(n, 1):
                            split(n + 1, 1 - slot)
                        if isinstance(n, int) and n == 0:
                            take_gate_row(1)
                        if inside(n, -1):
                            act.wait_ge(d_x1, n)
                            act.activation(sq[:], x1[:, 1 - slot, :], ACT.Square,
                                           accum_out=ss[:, 1 - slot, :]).then_inc(d_sq, 1)
                        if inside(n, -2):
                            t, r = n - 2, group(n, -2)
                            act.wait_ge(d_tr, 2 + t + 1)
                            act.wait_ge(d_lg, t + 1)
                            for k in range(NK):
                                op = act.activation(h2T[:, slot, k, :], trs[:, k * P:(k + 1) * P], ACT.Identity,
                                                    bias=modT[:, 3, k, r:r + 1], scale=scaleA[:, 1, k, r:r + 1])
                            op.then_inc(d_h2, 1)
                        if inside(n, -3):
                            t = n - 3
                            waits(act, (d_lg, 2 + t + 1))
                            act.activation(L[:, bass.ds(t, 1), :], lg[:, 0:E].unsqueeze(1), ACT.Copy).then_inc(d_lc, 1)

                    schedule(act, step)

                @block.vector
                def _(dve):
                    dve.sem_inc(d_clo, 2)
                    dve.sem_inc(d_gx, 2)
                    dve.memset(ones[:], 1.0).then_inc(d_ones, 1)
                    def split(m, slot):
                        dve.wait_ge(d_chi, 2 + m + 1)
                        dve.tensor_tensor(ca[1][:, slot, :, :], rawc[:, slot, :, :], ca[0][:, slot, :, :].bitcast(F32),
                                          ALU.subtract).then_inc(d_clo, 1)

                    split(0, 0)
                    for k in range(NK):
                        dve.wait_ge(d_hi, k + 1)
                        dve.tensor_tensor(wo[1][:, k, :], rawo[:, k, :], wo[0][:, k, :].bitcast(F32),
                                          ALU.subtract).then_inc(d_lo, 1)
                    dve.wait_ge(d_bcc, 1)

                    def step(n, slot):
                        if inside(n, 1):
                            split(n + 1, 1 - slot)
                        if inside(n, -1):
                            t, r, at = n - 1, group(n, -1), 1 - slot
                            if r == 1:
                                dve.wait_ge(d_bcc, 2)
                            dve.wait_ge(d_mm, 2 + t + 1)
                            dve.wait_ge(d_st[at], 16 * (t - at) + 32)
                            dve.tensor_tensor(x1[:, at, :], ops[at][:], gates[0][:, r, :],
                                              ALU.mult).then_inc(d_gx, 1)
                            dve.wait_ge(d_rs, t + 1)
                            dve.tensor_scalar(xn[:, at, :], x1[:, at, :], rs[:, at, :], None, ALU.mult).then_inc(d_xn, 1)

                    schedule(dve, step)

                @block.gpsimd
                def _(gp):
                    for r in range(2):
                        for k in range(NK):
                            op = gp.tensor_scalar(diag[:, r, k, :], ident[:], modT[:, 2, k, r:r + 1], None, ALU.mult)
                        op.then_inc(d_diag, 1)

                    def step(n, slot):
                        if inside(n, -1):
                            t, at = n - 1, 1 - slot
                            gp.wait_ge(d_x[at], 8 * (t - at) + 16)
                            gp.wait_ge(d_gx, 2 + t + 1)
                            gp.tensor_tensor(x1[:, at, :], x1[:, at, :], xt[:, at, :], ALU.add).then_inc(d_x1, 1)
                            waits(gp, (d_sq, t + 1))
                            gp.tensor_scalar(ss[:, at, :], ss[:, at, :], 1.0 / D, EPS, ALU.mult, ALU.add).then_inc(d_ms, 1)
                            gp.wait_ge(d_ms, t + 1)
                            gp.tensor_tensor(rs[:, at, :], ss[:, at, :], nhalf[:, 0:1], ALU.pow).then_inc(d_rs, 1)

                    schedule(gp, step)

        RING = 3
        G_, U_, D_ = 0, 1, 2
        raw = sb("rawW", [P, RING, 3, NK * W_STEP])
        wGU = [[sb(f"w{n}_{x}", [P, NK, W_STEP], F32R) for x in ("hi", "lo")] for n in "GU"]
        f_raw = [[sem(f"f_raw{n}{j}") for j in range(RING)] for n in "GUD"]
        f_hi, f_lo = [sem(f"f_hi{n}") for n in "GUD"], [sem(f"f_lo{n}") for n in "GUD"]
        USES = [len(range(j, STEPS, RING)) for j in range(RING)]
        LAST = [max(range(j, STEPS, RING)) for j in range(RING)]
        wg_ = io["w_gate"][0].rearrange("e (k p) f -> p e k f", p=P)
        wu_ = io["w_up"][0].rearrange("e (k p) f -> p e k f", p=P)
        wd_ = io["w_down"][0].rearrange("e (s f p) d -> p e s f d", p=P, f=2)

        def load(sp, kind, e, i):
            dst = raw[:, i % RING, kind, :]
            if kind == D_:
                dst, src = dst.rearrange("p (f d) -> p f d", f=2), wd_[:, bass.ds(e, 1), i, :, :]
                src = src.rearrange("p e f d -> p (e f) d")
            else:
                src = (wg_, wu_)[kind][:, bass.ds(e, 1), :, i * W_STEP:(i + 1) * W_STEP]
                dst, src = dst.rearrange("p (k f) -> p k f", k=NK), src.rearrange("p e k f -> p (e k) f")
            sp.dma_start(dst, src).then_inc(f_raw[kind][i % RING], 16)

        def raw_ready(eng, kind, e, i):
            eng.wait_ge(f_raw[kind][i % RING], 16 * (USES[i % RING] * e + i // RING + 1))

        def split_part(kind, i, half, part):
            a, b = half * NK * W_STEP // 2, (half + 1) * NK * W_STEP // 2
            if kind == D_:
                dst = wD[part][:, i % 2, half, :]
            else:
                dst = wGU[kind][part][:, half * NK // 2:(half + 1) * NK // 2, :].rearrange("p k f -> p (k f)")
            return dst, raw[:, i % RING, kind, a:b]

        def lo_half(eng, kind, e, i, half):
            eng.wait_ge(f_hi[kind], 2 * (STEPS * e + i) + half + 1)
            (hi, src), (lo, _) = split_part(kind, i, half, 0), split_part(kind, i, half, 1)
            eng.tensor_tensor(lo, src, hi.bitcast(F32), ALU.subtract).then_inc(f_lo[kind], 1)

        def hi_halves(act, kind, e, i, halves=(0, 1)):
            raw_ready(act, kind, e, i)
            for half in halves:
                dst, src = split_part(kind, i, half, 0)
                act.activation(dst, src, ACT.Copy).then_inc(f_hi[kind], 1)

        idxT = sb("idxT", [P, 48], I32)
        gT = sb("gT", [P, 48])
        with ExitStack() as c:
            mx = sb("mx", [P, T], F32, c)
            sm_ = sb("sm", [P, T], F32, c)
            affP = sb("affP", [P, TS // 2, 80], F32, c)
            top = sb("top", [80, N_S // 2], F32, c)
            vals = sb("topv", [80, P], F32, c)
            idxu = sb("topi", [80, P], U32, c)
            idxf = sb("idxf", [80, P], F32, c)
            v2, i2 = sb("v2", [E, P], F32, c), sb("i2", [E, P], F32, c)
            first = sb("first", [E, P], F32, c)
            tb = ps("tb", [80, 512], c)
            ti, tv = ps("ti", [P, 512], c), ps("tv", [P, 512], c)
            ones, diag = sb("onesE", [P, P], F32, c), sb("diagE", [P, 2, NK, P], F32, c)
            rows = ps("rows", [P, 2, D], c)
            e_v, e_exp, e_aff, e_tb, e_t, e_f, e_tt = (sem("e_v"), sem("e_exp"), sem("e_aff"), sem("e_tb"),
                                                            sem("e_t"), sem("e_f"), sem("e_tt"))
            e_diag, e_rows = sem("e_diag"), sem("e_rows")
            ROUNDS = CS // 8
            with nc.Block() as block:
                @block.scalar
                def _(act):
                    act.wait_ge(e_v, 2)
                    act.activation(L[:], L[:], ACT.Exp).then_inc(e_exp, 1)
                    for kind in (G_, U_):
                        hi_halves(act, kind, 0, 0)
                    act.wait_ge(e_rows, 1)
                    act.activation(gates[1][:], rows[:], ACT.Copy).then_inc(e_rows, 1)

                @block.gpsimd
                def _(gp):
                    gp.memset(ones[:], 1.0)
                    for r in range(2):
                        for k in range(NK):
                            op = gp.tensor_scalar(diag[:, r, k, :], ident[:], modT[:, 5, k, r:r + 1], None, ALU.mult)
                    op.then_inc(e_diag, 1)
                    for kind in (G_, U_):
                        for half in range(2):
                            lo_half(gp, kind, 0, 0, half)

                @block.tensor
                def _(pe):
                    pe.wait_ge(e_aff, 1)
                    for t in range(TS // 2):
                        mm = pe.transpose(tb[:, t * P:(t + 1) * P], affP[:, t, :], ident[:])
                    mm.then_inc(e_tb, 1)
                    pe.wait_ge(e_diag, 1)
                    for r in range(2):
                        for k in range(NK):
                            mm = pe.matmul(rows[:, r, k * P:(k + 1) * P], ones[:], diag[:, r, k, :], start=True, stop=True)
                    mm.then_inc(e_rows, 1)
                    pe.wait_ge(e_f, 1)
                    pe.transpose(ti[:, 0:48], idxf[0:48], ident[0:48, 0:48])
                    pe.transpose(tv[:, 0:48], vals[0:48], ident[0:48, 0:48]).then_inc(e_tt, 1)

                @block.vector
                def _(dve):
                    count = [0]

                    def own(op):
                        count[0] += 1
                        op.then_inc(e_v, 1)
                        dve.wait_ge(e_v, count[0])

                    own(dve.tensor_reduce(mx[:], L[:], AX.X, ALU.max))
                    own(dve.tensor_tensor(L[:], L[:], mx[:].unsqueeze(2).broadcast_to([P, T, E]), ALU.subtract))
                    own(dve.memset(affP[:], -1.0))
                    dve.wait_ge(e_exp, 1)
                    own(dve.tensor_reduce(sm_[:], L[:], AX.X, ALU.add))
                    own(dve.reciprocal(sm_[:], sm_[:]))
                    rcp = sm_[:].unsqueeze(2).broadcast_to([P, T, E])
                    for half, at in ((slice(0, TS // 2), 0), (slice(TS // 2, TS), 64)):
                        dve.tensor_tensor(affP[:, :, at:at + E], L[:, half, :], rcp[:, half, :], ALU.mult)
                    dve.tensor_tensor(affP[:, 0:TP, 32:48], L[:, TS:T, :], rcp[:, TS:T, :], ALU.mult).then_inc(e_aff, 1)
                    dve.wait_ge(e_tb, 1)
                    own(dve.tensor_copy(top[:], tb[:]))
                    for n in range(ROUNDS):
                        v = vals[:, 8 * n:8 * n + 8]
                        own(dve.max(v, top[:]))
                        own(dve.max_index(idxu[:, 8 * n:8 * n + 8], v, top[:]))
                        if n < ROUNDS - 1:
                            own(dve.match_replace(top[:], v, top[:], -1.0))
                    own(dve.tensor_copy(idxf[:], idxu[:]))
                    dve.tensor_scalar(idxf[32:48, :], idxf[32:48, :], float(N_S), None, ALU.add)
                    own(dve.tensor_scalar(idxf[64:80, :], idxf[64:80, :], float(N_S // 2), None, ALU.add))
                    dve.tensor_copy(v2[:], vals[64:80, ::-1])
                    own(dve.tensor_copy(i2[:], idxf[64:80, ::-1]))
                    dve.tensor_tensor(first[:], vals[0:E, :], v2[:], ALU.is_ge)
                    own(dve.tensor_tensor(idxf[0:E, :], idxf[0:E, :], i2[:], ALU.subtract))
                    own(dve.tensor_tensor(idxf[0:E, :], idxf[0:E, :], first[:], ALU.mult))
                    dve.tensor_tensor(idxf[0:E, :], idxf[0:E, :], i2[:], ALU.add)
                    dve.tensor_tensor(vals[0:E, :], vals[0:E, :], v2[:], ALU.max)
                    dve.tensor_copy(idxf[32:48, CP:2 * CP], idxf[32:48, 0:CP])
                    dve.tensor_copy(vals[32:48, CP:2 * CP], vals[32:48, 0:CP]).then_inc(e_f, 1)
                    dve.wait_ge(e_tt, 1)
                    dve.tensor_copy(idxT[:], ti[:, 0:48])
                    dve.tensor_copy(gT[:], tv[:, 0:48]).then_inc(e_t, 1)

                @block.sync
                def _(sp):
                    for i in range(RING):
                        for kind in (G_, U_, D_):
                            load(sp, kind, 0, i)

        with ExitStack() as c:
            wD = [sb(f"wD_{x}", [P, 2, 2, D], F32R, c) for x in ("hi", "lo")]
            X = sb("X", [P, NK, 2 * C], F32R, c)
            xm = sb("xm", [P, NK, C], F32, c)
            hid = sb("hid", [P, 2, 2, 2 * C], F32R, c)
            gl, ga, sg = sb("gl", [P, 2, C], F32, c), sb("ga", [P, 2, C], F32, c), sb("sg", [P, 2, C], F32, c)
            ul, ua, hf = sb("ul", [P, 2, C], F32, c), sb("ua", [P, 2, C], F32, c), sb("hf", [P, 2, C], F32, c)
            yp = sb("yp", [CP, D], F32, c)
            xg = [sb("xgS", [CS, D], F32, c), sb("xgP", [CP, D], F32, c)]
            ys = [sb("ysS", [CS, D], F32, c), sb("ysP", [CP, D], F32, c)]
            gi, si = sb("gi", [P, 2], I32, c), sb("si", [P, 2], I32, c)
            gc = sb("gc", [P, 2], F32, c)
            psG, psU = ps("psG", [P, 2, 512], c), ps("psU", [P, 2, 512], c)
            psS = ps("psS", [CS, 2, 512], c)
            psP = ps("psP", [2 * CP, 2, 512], c)
            XT = slice(2 * C, 3 * C)
            f_g, f_u, f_d = sem("f_g"), sem("f_u"), sem("f_d")
            f_gl, f_ul = sem("f_gl"), sem("f_ul")
            f_ga, f_ua = sem("f_ga"), sem("f_ua")
            f_sg, f_hf = sem("f_sg"), sem("f_hf")
            f_hh, f_hl = sem("f_hh"), sem("f_hl")
            f_gi, f_got = sem("f_gi"), sem("f_got")
            f_xt, f_xm = sem("f_xt"), sem("f_xm")
            f_xh, f_x = sem("f_xh"), sem("f_x")
            f_si, f_y = sem("f_si"), sem("f_y")
            f_sum, f_ys = sem("f_sum"), sem("f_ys")
            f_sc, f_free = sem("f_sc"), sem("f_free")
            f_tail = sem("f_tail")

            def pair(t, e):
                return t[:].rearrange("p (a e) -> p a e", e=E)[:, 0:3:2, bass.ds(e, 1)]

            def experts(eng, body):
                body(0, True, False)
                with eng.Fori(1, E - 1) as e:
                    body(e, False, False)
                body(E - 1, False, True)

            def following(e, i):
                return (e, i + 1) if i + 1 < STEPS else (e + 1, 0)

            with nc.Block() as block:
                @block.sync
                def _(sp):
                    sp.wait_ge(f_got, 32)

                    def body(e, first, last):
                        for i in range(STEPS):
                            s = STEPS * e + i
                            for kind in (G_, U_, D_):
                                if first and i < RING:
                                    continue
                                back = RING if i >= RING else STEPS + i - LAST[i]
                                sp.wait_ge(f_lo[kind], 2 * (s - back + 1))
                                load(sp, kind, e, i)

                    experts(sp, body)

                @block.tensor
                def _(pe):
                    pe.sem_inc(f_d, 2)

                    def gate_or_up(kind, out, e, i):
                        s = STEPS * e + i
                        for k in range(NK):
                            if k in (0, NK // 2):
                                pe.wait_ge(f_lo[kind], 2 * s + (1 if k == 0 else 2))
                            for f in range(2):
                                hi, lo = (wGU[kind][x][:, k, f * P:(f + 1) * P] for x in range(2))
                                pe.matmul(out[:, f, 0:2 * C], hi, X[:, k, :], start=(k == 0), stop=False,
                                          skip_group_check=True)
                                mm = pe.matmul(out[:, f, 0:C], lo, X[:, k, 0:C], start=False, stop=(k == NK - 1),
                                               skip_group_check=True)
                        return mm

                    def down(e, i):
                        s = STEPS * e + i
                        pe.wait_ge(f_hl, 1 + s + 1)
                        if i == 0:
                            pe.wait_ge(f_y, e + 1)
                        for f in range(2):
                            pe.wait_ge(f_lo[D_], 2 * s + f + 1)
                            h = hid[:, i % 2, f, :]
                            latent_hi, latent_lo, context_hi, context = (h[:, 0:CS], h[:, C + CP:2 * C],
                                                                         h[:, CS:C], h[:, CS:C + CP])
                            for w, out, x in ((0, psS, latent_hi), (0, psS, latent_lo), (0, psP, context),
                                              (1, psS, latent_hi), (1, psP[0:CP], context_hi)):
                                for half in range(2):
                                    mm = pe.matmul(out[:, half, :], x, wD[w][:, i % 2, f, half * 512:(half + 1) * 512],
                                                   start=(i == 0 and f == 0 and w == 0 and x is not latent_lo),
                                                   stop=(i == STEPS - 1 and f == 1 and w == 1), skip_group_check=True)
                        mm.then_inc(f_d, 1)

                    def transpose_rows(k, bank):
                        out = psU[:, bank, XT]
                        pe.transpose(out[:, 0:CS], xg[0][:, k * P:(k + 1) * P], ident[:])
                        return pe.transpose(out[:, CS:C], xg[1][:, k * P:(k + 1) * P], ident[0:CP, 0:CP])

                    pe.wait_ge(f_got, 32)
                    for k in range(NK):
                        if k >= 2:
                            pe.wait_ge(f_xm, k - 1)
                        transpose_rows(k, k % 2).then_inc(f_xt, 1)

                    def body(e, first, last):
                        for i in range(STEPS):
                            s = STEPS * e + i
                            if i == 0:
                                pe.wait_ge(f_x, 2 * e + 2)
                            pe.wait_ge(f_ga, s + 1)
                            gate_or_up(G_, psG, e, i).then_inc(f_g, 1)
                            pe.wait_ge(f_ua, s + 1)
                            if i > STEPS - NK and not last:
                                pe.wait_ge(f_xm, NK * (e + 1) + i - (STEPS - NK))
                            if i == 0:
                                pe.wait_ge(f_xm, NK * (e + 1))
                            mm = gate_or_up(U_, psU, e, i)
                            if i >= STEPS - NK and not last:
                                if i == STEPS - NK:
                                    pe.wait_ge(f_got, 32 * (e + 2))
                                mm = transpose_rows(i - (STEPS - NK), 0)
                            mm.then_inc(f_u, 1)
                            if i:
                                down(e, i - 1)
                        down(e, STEPS - 1)

                    experts(pe, body)

                @block.scalar
                def _(act):
                    act.sem_inc(f_y, 1)

                    def x_hi(e):
                        act.wait_ge(f_xm, NK * (e + 1))
                        for half in range(2):
                            a, b = half * NK // 2, (half + 1) * NK // 2
                            act.activation(X[:, a:b, 0:C], xm[:, a:b, :], ACT.Copy).then_inc(f_xh, 1)

                    def take_y(e):
                        act.wait_ge(f_d, 2 + STEPS * e)
                        act.wait_ge(f_si, e)
                        for dst, src, scale in ((ys[0], psS[:], gc[:, 0:1]), (ys[1], psP[0:CP], 1.0),
                                                (yp, psP[CP:2 * CP], 1.0)):
                            op = act.activation(dst[:].rearrange("p (a d) -> p a d", a=2), src, ACT.Copy, scale=scale)
                        op.then_inc(f_y, 1)

                    x_hi(0)

                    def body(e, first, last):
                        for i in range(STEPS):
                            s, n = STEPS * e + i, following(e, i)
                            end = last and i == STEPS - 1
                            act.wait_ge(f_g, s + 1)
                            act.activation(gl[:], psG[:, :, C:2 * C], ACT.Copy).then_inc(f_gl, 1)
                            if not end:
                                hi_halves(act, G_, *n)
                            act.wait_ge(f_ga, 1 + s + 1)
                            act.activation(sg[:], ga[:], ACT.Silu).then_inc(f_sg, 1)
                            act.wait_ge(f_u, s + 1)
                            act.activation(ul[:], psU[:, :, C:2 * C], ACT.Copy).then_inc(f_ul, 1)
                            if not end:
                                hi_halves(act, U_, *n, halves=(0,) if i == STEPS - 1 else (0, 1))
                            act.wait_ge(f_hf, s + 1)
                            act.activation(hid[:, i % 2, :, 0:C], hf[:], ACT.Copy).then_inc(f_hh, 1)
                            if i == STEPS - 1 and not last:
                                x_hi(e + 1)
                                hi_halves(act, U_, *n, halves=(1,))
                            if i == 0 and not first:
                                take_y(e)

                    experts(act, body)
                    take_y(E)

                @block.vector
                def _(dve):
                    for sm in (f_ga, f_ua, f_hl):
                        dve.sem_inc(sm, 1)
                    dve.tensor_copy(gi[:].unsqueeze(2), pair(idxT, 0)).then_inc(f_gi, 1)

                    def x_mod(k, bank):
                        src = psU[:, bank, XT]
                        for r, a, b in ((0, 0, CS), (1, CS, C)):
                            op = dve.tensor_scalar(xm[:, k, a:b], src[:, a:b], scaleA[:, 1, k, r:r + 1],
                                                   modT[:, 3, k, r:r + 1], ALU.mult, ALU.add)
                        return op

                    def x_lo(e):
                        for half in range(2):
                            dve.wait_ge(f_xh, 2 * e + half + 1)
                            a, b = half * NK // 2, (half + 1) * NK // 2
                            dve.tensor_tensor(X[:, a:b, C:2 * C], xm[:, a:b, :], X[:, a:b, 0:C].bitcast(F32),
                                              ALU.subtract).then_inc(f_x, 1)

                    def for_scatter(e):
                        dve.wait_ge(f_free, e)
                        dve.tensor_copy(si[:].unsqueeze(2), pair(idxT, e - 1))
                        dve.tensor_copy(gc[:].unsqueeze(2), pair(gT, e - 1)).then_inc(f_si, 1)

                    def down_hi(e, i, s):
                        dve.wait_ge(f_d, s + (1 if i else 2))
                        raw_ready(dve, D_, e, i)
                        for half in range(2):
                            dst, src = split_part(D_, i, half, 0)
                            dve.tensor_copy(dst, src).then_inc(f_hi[D_], 1)

                    for k in range(NK):
                        dve.wait_ge(f_xt, k + 1)
                        x_mod(k, k % 2).then_inc(f_xm, 1)
                    x_lo(0)

                    def body(e, first, last):
                        for i in range(STEPS):
                            s, n = STEPS * e + i, following(e, i)
                            end = last and i == STEPS - 1
                            if i == 0 and not last:
                                dve.tensor_copy(gi[:].unsqueeze(2), pair(idxT, e + 1)).then_inc(f_gi, 1)
                            dve.wait_ge(f_gl, s + 1)
                            dve.tensor_tensor(ga[:], psG[:, :, 0:C], gl[:], ALU.add).then_inc(f_ga, 1)
                            if i == 0 and not first:
                                for_scatter(e)
                            final = i == STEPS - 1
                            if final:
                                down_hi(e, i, s)
                            for half in range(1 if final else 2):
                                if not end:
                                    lo_half(dve, G_, *n, half)
                            if not final:
                                down_hi(e, i, s)
                            dve.wait_ge(f_ul, s + 1)
                            dve.tensor_tensor(ua[:], psU[:, :, 0:C], ul[:], ALU.add).then_inc(f_ua, 1)
                            dve.wait_ge(f_ua, 1 + s + 1)
                            dve.wait_ge(f_sg, s + 1)
                            dve.wait_ge(f_hl, s + 1)
                            dve.tensor_tensor(hf[:], sg[:], ua[:], ALU.mult).then_inc(f_hf, 1)
                            if not end:
                                if final:
                                    lo_half(dve, G_, *n, 1)
                                else:
                                    for half in range(2 if i == 0 else 1):
                                        lo_half(dve, U_, *n, half)
                            dve.wait_ge(f_hh, s + 1)
                            for dst, a, b in ((C, CS, C), (C + CP, 0, CS)):
                                op = dve.tensor_tensor(hid[:, i % 2, :, dst:dst + b - a], hf[:, :, a:b],
                                                       hid[:, i % 2, :, a:b].bitcast(F32), ALU.subtract)
                            op.then_inc(f_hl, 1)
                            if i >= STEPS - NK and not last:
                                x_mod(i - (STEPS - NK), 0).then_inc(f_xm, 1)
                            if final and not last:
                                x_lo(e + 1)
                            if not end and i:
                                for half in range(0 if final else 1, 2):
                                    lo_half(dve, U_, *n, half)

                    experts(dve, body)
                    for_scatter(E)
                    dve.wait_ge(f_y, 1 + E)
                    dve.tensor_tensor(ys[1][:], ys[1][:], yp[:], ALU.add).then_inc(f_tail, 1)
                    dve.tensor_tensor(ys[0][:], ys[0][:], gates[1][:, 0, :], ALU.mult)
                    dve.wait_ge(f_tail, 1)
                    dve.scalar_tensor_tensor(ys[1][:], ys[1][:], gc[0:CP, 1:2], gates[1][0:CP, 1, :],
                                             ALU.mult, ALU.mult).then_inc(f_tail, 1)

                @block.gpsimd
                def _(gp):
                    gp.sem_inc(f_free, 1)

                    def gather(e):
                        waits(gp, (f_gi, e + 1))
                        for r, n in ((0, CS), (1, CP)):
                            gp.indirect_dma_start(xg[r][:], None, xn2[:], bass.IndirectOffsetOnAxis(ap=gi[0:n, r:r + 1], axis=0)
                                                  ).then_inc(f_got, 16)

                    def finish_context(e):
                        gp.wait_ge(f_y, 1 + e)
                        gp.tensor_tensor(ys[1][:], ys[1][:], yp[:], ALU.add).then_inc(f_sum, 1)
                        waits(gp, (f_sum, 2 * e - 1))
                        gp.tensor_scalar(ys[1][:], ys[1][:], gc[0:CP, 1:2], None, ALU.mult).then_inc(f_sum, 1)

                    def scatter_rows():
                        for r, n in ((0, CS), (1, CP)):
                            gp.indirect_dma_start(acc[:], bass.IndirectOffsetOnAxis(ap=si[0:n, r:r + 1], axis=0), ys[r][:], None,
                                                  compute_op=ALU.add).then_inc(f_sc, 16)

                    def scatter(e):
                        gp.wait_ge(f_sum, 2 * e)
                        gp.tensor_tensor(ys[1][:], ys[1][:], gates[1][0:CP, 1, :], ALU.mult)
                        gp.tensor_tensor(ys[0][:], ys[0][:], gates[1][:, 0, :], ALU.mult).then_inc(f_ys, 1)
                        waits(gp, (f_ys, e))
                        scatter_rows()

                    gather(0)

                    def body(e, first, last):
                        for i in range(STEPS):
                            if i == 0 and not last:
                                gp.wait_ge(f_xt, NK)
                                if not first:
                                    gp.wait_ge(f_u, STEPS * e)
                                gather(e + 1)
                            for half in range(2):
                                lo_half(gp, D_, e, i, half)
                            if i == 0 and not first:
                                finish_context(e)
                            if i == 1 and not first:
                                scatter(e)
                            if i == 3 and not first:
                                gp.wait_ge(f_sc, 32 * e)
                                gp.sem_inc(f_free, 1)

                    experts(gp, body)
                    gp.wait_ge(f_tail, 2)
                    scatter_rows()
                    gp.wait_ge(f_sc, 32 * E)

        with ExitStack() as c:
            xf = sb("xf", [P, T, D], F32, c)
            gf = sb("gf", [P, D], F32, c)
            sq = sb("sqG", [P, 2, D], F32, c)
            ss, rs = sb("ssG", [P, T], F32, c), sb("rsG", [P, T], F32, c)
            g_g, g_x = sem("g_g"), a_x
            g_sq, g_ms, g_rs, g_y, g_out = sem("g_sq"), sem("g_ms"), sem("g_rs"), sem("g_y"), sem("g_out")
            with nc.Block() as block:
                @block.sync
                def _(sp):
                    for t in range(T):
                        sp.dma_start(xf[:, t, :], acc[t * P:(t + 1) * P, :]).then_inc(g_x[t], 16)
                        if t == 0:
                            sp.dma_start(gf[:], io["final_g"].rearrange("(a d) -> a d", a=1).broadcast_to([P, D])
                                         ).then_inc(g_g, 16)
                    for t in range(T):
                        sp.wait_ge(g_y, t + 1)
                        dst = (io["y_sample"][0, t * P:(t + 1) * P, :] if t < TS else
                               io["y_prompt"][0, (t - TS) * P:(t - TS + 1) * P, :])
                        sp.dma_start(dst, xf[:, t, :]).then_inc(g_out, 16)
                    sp.wait_ge(g_out, 16 * T)

                @block.scalar
                def _(act):
                    for t in range(T):
                        act.wait_ge(g_x[t], 32)
                        if t >= 2:
                            act.wait_ge(g_sq, t - 1)
                        act.activation(sq[:, t % 2, :], xf[:, t, :], ACT.Square, accum_out=ss[:, t:t + 1]).then_inc(g_sq, 1)

                @block.gpsimd
                def _(gp):
                    for t in range(T):
                        gp.wait_ge(g_sq, t + 1)
                        gp.tensor_scalar(ss[:, t:t + 1], ss[:, t:t + 1], 1.0 / D, EPS, ALU.mult, ALU.add).then_inc(g_ms, 1)
                        gp.wait_ge(g_ms, t + 1)
                        gp.tensor_tensor(rs[:, t:t + 1], ss[:, t:t + 1], nhalf[:, 0:1], ALU.pow).then_inc(g_rs, 1)

                @block.vector
                def _(dve):
                    dve.wait_ge(g_g, 16)
                    for t in range(T):
                        dve.wait_ge(g_rs, t + 1)
                        dve.scalar_tensor_tensor(xf[:, t, :], xf[:, t, :], rs[:, t:t + 1], gf[:], ALU.mult,
                                                 ALU.mult).then_inc(g_y, 1)


_OUT = [("y_prompt", (1, N_P, D)), ("y_sample", (1, N_S, D)), ("state_out", (1, 1, 2, H, P, P))]


def kernel(x_prompt, x_sample, state_ret, c, c_ctx, norm1_g, norm2_g, final_g, w_mod, b_mod,
           w_in, w_fmix, w_out, w_router, w_gate, w_up, w_down):
    import concourse.bacc as bacc
    from concourse.bass_utils import run_bass_kernel_spmd

    ins = dict(x_prompt=x_prompt, x_sample=x_sample, state_ret=state_ret, c=c, c_ctx=c_ctx, norm1_g=norm1_g,
               norm2_g=norm2_g, final_g=final_g, w_mod=w_mod, b_mod=b_mod, w_in=w_in, w_fmix=w_fmix, w_out=w_out,
               w_router=w_router, w_gate=w_gate, w_up=w_up, w_down=w_down)
    arrays = {f"in_{k}": np.asarray(v) for k, v in {**ins, **tables()}.items()}
    nc = bacc.Bacc("TRN2", target_bir_lowering=False, num_devices=1)
    io = {k[3:]: nc.dram_tensor(k, v.shape, mybir.dt.from_np(v.dtype), kind="ExternalInput").ap() for k, v in arrays.items()}
    for k, shape in _OUT:
        io[k] = nc.dram_tensor(k, shape, F32, kind="ExternalOutput").ap()
    build(nc, io)
    nc.finalize()
    res = run_bass_kernel_spmd(nc, [arrays], core_ids=[0]).results[0]
    return res["y_prompt"], res["y_sample"], res["state_out"]
```
